# Optimizing a Trainium2 kernel written in Bass

```python
import math
import jax, jax.numpy as jnp
from jax import lax
import numpy as np

D_MODEL = 1024
BATCH = 1
SEQ = 1024
DEPTH = 1

CONV_CH = 512
CONV_KERNEL = 31
ATTN_HEADS = 8
ATTN_HEAD_DIM = 64
ATTN_W = ATTN_HEADS * ATTN_HEAD_DIM
SSD_HEADS = 8
SSD_HEAD_DIM = 64
SSD_W = SSD_HEADS * SSD_HEAD_DIM
SSD_GROUPS = 2
SSD_STATE = 64
SSD_CONV = 4
SSD_CONV_CH = SSD_W + 2 * SSD_GROUPS * SSD_STATE
SSD_CHUNK = 128
Q_BLOCK = 128
D_MIX = CONV_CH + ATTN_W + SSD_W
IN_SIZES = (2 * CONV_CH, ATTN_W, ATTN_W, ATTN_W, ATTN_HEADS,
            SSD_W, SSD_W, SSD_GROUPS * SSD_STATE, SSD_GROUPS * SSD_STATE, SSD_HEADS)
D_IN = sum(IN_SIZES)
MOE_GROUPS = 4
EXPERTS_PER_GROUP = 4
N_EXPERTS = MOE_GROUPS * EXPERTS_PER_GROUP
TOP_K_INNER = 2
D_EXPERT = 512
EPS = 1e-6

kernel_name = "hybrid_conv_fox_ssd_hmoe"

def rmsnorm(x, g):
    xf = x.astype(jnp.float32)
    y = xf * lax.rsqrt(jnp.mean(xf * xf, axis=-1, keepdims=True) + EPS)
    return (y * g.astype(jnp.float32)).astype(x.dtype)

def layernorm(x, g, b):
    xf = x.astype(jnp.float32)
    mu = jnp.mean(xf, axis=-1, keepdims=True)
    var = jnp.mean(jnp.square(xf - mu), axis=-1, keepdims=True)
    y = (xf - mu) * lax.rsqrt(var + EPS) * g.astype(jnp.float32) + b.astype(jnp.float32)
    return y.astype(x.dtype)

def causal_depthwise_conv(x, w, b):
    K, C = w.shape
    y = lax.conv_general_dilated(
        x, w[:, None, :].astype(x.dtype), window_strides=(1,), padding=[(K - 1, 0)],
        dimension_numbers=("NWC", "WIO", "NWC"), feature_group_count=C)
    return y + b.astype(x.dtype)

def split_cols(u, sizes):
    offs = np.cumsum(sizes)[:-1].tolist()
    return jnp.split(u, offs, axis=-1)

def conformer_conv(u, dw_w, dw_b, ln_g, ln_b):
    a, gate = jnp.split(u, 2, axis=-1)
    h = a * jax.nn.sigmoid(gate)
    h = causal_depthwise_conv(h, dw_w, dw_b)
    h = layernorm(h, ln_g, ln_b)
    return jax.nn.silu(h)

def forgetting_attention(q, k, v, f_logit):
    Bn, L, _ = q.shape
    scale = ATTN_HEAD_DIM ** -0.5
    q = q.reshape(Bn, L, ATTN_HEADS, ATTN_HEAD_DIM) * scale
    k = k.reshape(Bn, L, ATTN_HEADS, ATTN_HEAD_DIM)
    v = v.reshape(Bn, L, ATTN_HEADS, ATTN_HEAD_DIM)
    log_f = jax.nn.log_sigmoid(f_logit.astype(jnp.float32))
    cum = jnp.transpose(jnp.cumsum(log_f, axis=1), (0, 2, 1))
    outs = []
    for i in range(L // Q_BLOCK):
        q0 = i * Q_BLOCK
        end = q0 + Q_BLOCK
        s = jnp.einsum('bqhd,bkhd->bhqk', q[:, q0:end], k[:, :end]).astype(jnp.float32)
        s = s + cum[:, :, q0:end, None] - cum[:, :, None, :end]
        qpos = q0 + jnp.arange(Q_BLOCK)
        kpos = jnp.arange(end)
        s = jnp.where(kpos[None, :] <= qpos[:, None], s, -jnp.inf)
        p = jax.nn.softmax(s, axis=-1)
        outs.append(jnp.einsum('bhqk,bkhd->bqhd', p.astype(v.dtype), v[:, :end]))
    o = jnp.concatenate(outs, axis=1)
    return o.reshape(Bn, L, ATTN_W)

def ssd_chunked(x, a, Bm, Cm):
    Bn, L, H, P = x.shape
    G, N = Bm.shape[2], Bm.shape[3]
    R = H // G
    T = SSD_CHUNK
    nc = L // T
    x = x.reshape(Bn, nc, T, G, R, P)
    a = a.reshape(Bn, nc, T, G, R)
    Bm = Bm.reshape(Bn, nc, T, G, N)
    Cm = Cm.reshape(Bn, nc, T, G, N)
    a_cum = jnp.cumsum(a, axis=2)
    seg = a_cum[:, :, :, None] - a_cum[:, :, None, :]
    causal = jnp.tril(jnp.ones((T, T), dtype=bool))[None, None, :, :, None, None]
    Lmat = jnp.exp(jnp.where(causal, seg, -jnp.inf))
    CB = jnp.einsum('bctgn,bcsgn->bctsg', Cm, Bm)
    y_diag = jnp.einsum('bctsgr,bcsgrp->bctgrp', CB[..., None] * Lmat, x)
    decay_to_end = jnp.exp(a_cum[:, :, -1:] - a_cum)
    states = jnp.einsum('bctgn,bctgrp->bcgrpn', Bm, x * decay_to_end[..., None])
    chunk_decay = jnp.exp(a_cum[:, :, -1])

    def step(h, inp):
        s_c, d_c = inp
        return h * d_c[..., None, None] + s_c, h

    h0 = jnp.zeros((Bn, G, R, P, N), dtype=states.dtype)
    _, h_prev = lax.scan(step, h0, (jnp.moveaxis(states, 1, 0), jnp.moveaxis(chunk_decay, 1, 0)))
    h_prev = jnp.moveaxis(h_prev, 0, 1)
    y_off = jnp.einsum('bctgn,bcgrpn->bctgrp', Cm, h_prev) * jnp.exp(a_cum)[..., None]
    return (y_diag + y_off).reshape(Bn, L, H, P)

def ssd_mixer(z, xs, Bm, Cm, dt_raw, conv_w, conv_b, dt_bias, A_log, D_skip, norm_g):
    Bn, L, _ = xs.shape
    xbc = jax.nn.silu(causal_depthwise_conv(jnp.concatenate([xs, Bm, Cm], axis=-1), conv_w, conv_b))
    xs, Bm, Cm = split_cols(xbc, (SSD_W, SSD_GROUPS * SSD_STATE, SSD_GROUPS * SSD_STATE))
    x = xs.reshape(Bn, L, SSD_HEADS, SSD_HEAD_DIM).astype(jnp.float32)
    Bm = Bm.reshape(Bn, L, SSD_GROUPS, SSD_STATE).astype(jnp.float32)
    Cm = Cm.reshape(Bn, L, SSD_GROUPS, SSD_STATE).astype(jnp.float32)
    dt = jax.nn.softplus(dt_raw.astype(jnp.float32) + dt_bias.astype(jnp.float32))
    A = -jnp.exp(A_log.astype(jnp.float32))
    y = ssd_chunked(x * dt[..., None], dt * A, Bm, Cm)
    y = y + x * D_skip.astype(jnp.float32)[:, None]
    y = y.reshape(Bn, L, SSD_W).astype(z.dtype)
    return rmsnorm(y * jax.nn.silu(z), norm_g)

def hierarchical_moe(x, wg, bg, we, be, w_gate, w_up, w_down):
    Bn, L, _ = x.shape
    g_prob = jax.nn.softmax((x @ wg).astype(jnp.float32) + bg.astype(jnp.float32), axis=-1)
    g_val, g_idx = lax.top_k(g_prob, 1)
    e_logits = ((x @ we).astype(jnp.float32) + be.astype(jnp.float32)).reshape(
        Bn, L, MOE_GROUPS, EXPERTS_PER_GROUP)
    e_sel = jnp.take_along_axis(e_logits, g_idx[..., None], axis=2)[:, :, 0]
    e_val, e_idx = lax.top_k(e_sel, TOP_K_INNER)
    e_w = jax.nn.softmax(e_val, axis=-1) * g_val
    expert_id = g_idx * EXPERTS_PER_GROUP + e_idx
    combine = jnp.sum(jax.nn.one_hot(expert_id, N_EXPERTS, dtype=jnp.float32) * e_w[..., None], axis=-2)
    combine = combine.astype(x.dtype)
    out = jnp.zeros_like(x)
    for e in range(N_EXPERTS):
        h = jax.nn.silu(x @ w_gate[e]) * (x @ w_up[e])
        out = out + combine[..., e:e + 1] * (h @ w_down[e])
    return out

def setup_inputs(seed: int = 0) -> dict:
    key = jax.random.key(seed)
    ks = iter(jax.random.split(key, 32))
    nrm = lambda shape, s: jax.random.normal(next(ks), shape, jnp.float32) * s
    x = nrm((BATCH, SEQ, D_MODEL), 1.0)
    norm_mix = 1.0 + nrm((DEPTH, D_MODEL), 0.02)
    w_in = nrm((DEPTH, D_MODEL, D_IN), D_MODEL ** -0.5)
    conv_dw_w = nrm((DEPTH, CONV_KERNEL, CONV_CH), CONV_KERNEL ** -0.5)
    conv_dw_b = nrm((DEPTH, CONV_CH), 0.01)
    conv_ln_g = 1.0 + nrm((DEPTH, CONV_CH), 0.02)
    conv_ln_b = nrm((DEPTH, CONV_CH), 0.01)
    fgate_b = jax.random.uniform(next(ks), (DEPTH, ATTN_HEADS), jnp.float32, 1.0, 6.0)
    ssd_conv_w = nrm((DEPTH, SSD_CONV, SSD_CONV_CH), SSD_CONV ** -0.5)
    ssd_conv_b = nrm((DEPTH, SSD_CONV_CH), 0.01)
    u = jax.random.uniform(next(ks), (DEPTH, SSD_HEADS), jnp.float32)
    dt0 = jnp.exp(u * (math.log(0.1) - math.log(0.001)) + math.log(0.001))
    ssd_dt_bias = dt0 + jnp.log(-jnp.expm1(-dt0))
    ssd_A_log = jnp.log(jax.random.uniform(next(ks), (DEPTH, SSD_HEADS), jnp.float32, 1.0, 16.0))
    ssd_D = 1.0 + nrm((DEPTH, SSD_HEADS), 0.1)
    ssd_norm_g = 1.0 + nrm((DEPTH, SSD_W), 0.02)
    w_out = nrm((DEPTH, D_MIX, D_MODEL), D_MIX ** -0.5)
    norm_ffn = 1.0 + nrm((DEPTH, D_MODEL), 0.02)
    router_group_w = nrm((DEPTH, D_MODEL, MOE_GROUPS), D_MODEL ** -0.5)
    router_group_b = nrm((DEPTH, MOE_GROUPS), 0.01)
    router_expert_w = nrm((DEPTH, D_MODEL, N_EXPERTS), D_MODEL ** -0.5)
    router_expert_b = nrm((DEPTH, N_EXPERTS), 0.01)
    expert_w_gate = nrm((DEPTH, N_EXPERTS, D_MODEL, D_EXPERT), D_MODEL ** -0.5)
    expert_w_up = nrm((DEPTH, N_EXPERTS, D_MODEL, D_EXPERT), D_MODEL ** -0.5)
    expert_w_down = nrm((DEPTH, N_EXPERTS, D_EXPERT, D_MODEL), D_EXPERT ** -0.5)
    norm_final = 1.0 + nrm((D_MODEL,), 0.02)
    return {"x": x, "norm_mix": norm_mix, "w_in": w_in, "conv_dw_w": conv_dw_w, "conv_dw_b": conv_dw_b,
            "conv_ln_g": conv_ln_g, "conv_ln_b": conv_ln_b, "fgate_b": fgate_b, "ssd_conv_w": ssd_conv_w,
            "ssd_conv_b": ssd_conv_b, "ssd_dt_bias": ssd_dt_bias, "ssd_A_log": ssd_A_log, "ssd_D": ssd_D,
            "ssd_norm_g": ssd_norm_g, "w_out": w_out, "norm_ffn": norm_ffn, "router_group_w": router_group_w,
            "router_group_b": router_group_b, "router_expert_w": router_expert_w,
            "router_expert_b": router_expert_b, "expert_w_gate": expert_w_gate, "expert_w_up": expert_w_up,
            "expert_w_down": expert_w_down, "norm_final": norm_final}

def reference(x, norm_mix, w_in, conv_dw_w, conv_dw_b, conv_ln_g, conv_ln_b, fgate_b, ssd_conv_w,
              ssd_conv_b, ssd_dt_bias, ssd_A_log, ssd_D, ssd_norm_g, w_out, norm_ffn, router_group_w,
              router_group_b, router_expert_w, router_expert_b, expert_w_gate, expert_w_up,
              expert_w_down, norm_final):
    for l in range(DEPTH):
        h = rmsnorm(x, norm_mix[l])
        u = h @ w_in[l]
        (u_conv, q, k, v, f_logit, z, xs, Bm, Cm, dt_raw) = split_cols(u, IN_SIZES)
        y_conv = conformer_conv(u_conv, conv_dw_w[l], conv_dw_b[l], conv_ln_g[l], conv_ln_b[l])
        y_attn = forgetting_attention(q, k, v, f_logit + fgate_b[l].astype(f_logit.dtype))
        y_ssd = ssd_mixer(z, xs, Bm, Cm, dt_raw, ssd_conv_w[l], ssd_conv_b[l], ssd_dt_bias[l],
                          ssd_A_log[l], ssd_D[l], ssd_norm_g[l])
        y = jnp.concatenate([y_conv, y_attn.astype(x.dtype), y_ssd], axis=-1) @ w_out[l]
        x = x + y.astype(x.dtype)
        hf = rmsnorm(x, norm_ffn[l])
        x = x + hierarchical_moe(hf, router_group_w[l], router_group_b[l], router_expert_w[l],
                                 router_expert_b[l], expert_w_gate[l], expert_w_up[l],
                                 expert_w_down[l]).astype(x.dtype)
    return rmsnorm(x, norm_final)


_drawn_inputs = setup_inputs


def setup_inputs(seed=0):
    import zlib

    import numpy as np

    out = dict(_drawn_inputs(seed))
    spreads = {}
    factors = {'conv_dw_b': 4.044,
     'conv_ln_g': 14.751,
     'conv_ln_b': 31.654,
     'ssd_conv_b': 3.861,
     'ssd_norm_g': 11.515,
     'router_group_b': 25.272,
     'router_expert_b': 30.02,
     'norm_final': 8.423,
     'norm_ffn': 6.458}
    for name, (base, spread) in spreads.items():
        noise = np.random.default_rng([zlib.crc32(name.encode()), seed]).standard_normal(out[name].shape)
        drawn = base * np.exp(spread * noise) if base else spread * noise
        out[name] = __import__('jax').numpy.asarray(drawn.astype(out[name].dtype))
    for name, factor in factors.items():
        out[name] = (out[name] * factor).astype(out[name].dtype)
    return out
```

```python
from contextlib import ExitStack

import concourse.bass as bass
from concourse import mybir

F32 = mybir.dt.float32
BF16 = mybir.dt.bfloat16
F32R = mybir.dt.float32r
I32 = mybir.dt.int32
ALU = mybir.AluOpType
ACT = mybir.ActivationFunctionType
AX_X = mybir.AxisListType.X

P = 128
D = 1024
T = 1024
NT = T // P
KT = D // P
CONV = 512
CONV_K = 31
HEADS = 8
HD = 64
SW = 512
SCONV_K = 4
BIG = 1.0e30
WO_RING = 4
PIECES_OF_UNIT = (4, 4, 4, 4, 3, 3, 2, 3, 3, 2)
EPS = 1e-6
NG = 4
EPG = 4
NE = NG * EPG
FE = 512
SLOTS = 2 * T + NE * P
NB = SLOTS // P

C_A, C_GATE, C_Q, C_K, C_V = 0, 512, 1024, 1536, 2048
C_F, C_Z, C_XBC, C_DT = 2560, 2568, 3080, 3848


def trunk(nc, A, out):
    ctx = ExitStack()
    with ctx:
        def sb(name, shape, dt=F32):
            return ctx.enter_context(nc.sbuf_tensor(name, shape, dt))

        count = {}

        def sem(name):
            s = ctx.enter_context(nc.semaphore(name))
            count[name] = 0
            return (name, s)

        def sig(ins, s, n=1):
            ins.then_inc(s[1], n)
            count[s[0]] += n
            return count[s[0]]

        ident = sb("ident", [P, P])
        identb = sb("identb", [P, P], BF16)
        ones = sb("ones", [P, P])
        tri_le = sb("tri_le", [P, 4 * P])
        tri_gt = sb("tri_gt", [P, P])
        tri_lt = sb("tri_lt", [P, P], BF16)
        ones_b = sb("ones_b", [P, P], BF16)
        negmask = sb("negmask", [P, P], BF16)
        iota_j = sb("iota_j", [P, P])
        tok_idx = sb("tok_idx", [P, NT])
        thr = sb("thr", [P, NT - 1])
        rev4 = sb("rev4", [P, 4])
        eps = sb("eps", [P, 1])
        warm = sb("warm", [P, 1])

        convp = sb("convp", [P, 4, CONV_K + 3])
        sconvp = sb("sconvp", [P, 6, SCONV_K + 1])
        fdb = sb("fdb", [P, 16])
        alog = sb("alog", [P, HEADS])
        dskip = sb("dskip", [P, HEADS])
        sng = sb("sng", [P, SW])
        rb = sb("rb", [P, NG + NE])
        wr = sb("wr", [P, KT, NG + NE])

        ssq = sb("ssq", [P, NT])
        rms = sb("rms", [P, NT])
        rstd = sb("rstd", [P, NT])

        with nc.sbuf_tensor("area_ab", [P, 2 * 12288 + 256], F32) as area_ab:
            pass
        w_hi = sb("w_hi", [P, 12288], F32R)
        w_lo = sb("w_lo", [P, 12288], F32R)
        sb("area_ab_rest", [P, 256])
        area_b, area_a = area_ab[:, 0:12288], area_ab[:, 12288:2 * 12288 + 256]
        with nc.sbuf_tensor("area_c", [P, 4096], F32) as area_c:
            pass
        xT_hi = sb("xT_hi", [P, D], F32R)
        xT_lo = sb("xT_lo", [P, D], F32R)
        hT_hi = sb("hT_hi", [P, FE], F32R)
        hT_lo = sb("hT_lo", [P, FE], F32R)
        sb("area_c_rest", [P, D])
        with nc.sbuf_tensor("area_d", [P, 15400], F32) as area_d:
            pass
        sb("area_d_x1", [P, T // P * D])
        y_ring = sb("y_ring", [P, 2 * WO_RING * 3 * P], F32R)
        sb("area_d_rest", [P, 15400 - T // P * D - 2 * WO_RING * 3 * P])
        area_e = sb("area_e", [P, 4 * (CONV_K - 1 + T)])
        small = sb("small", [P, 1220])

        def view(area, at, *dims):
            n = 1
            for d in dims:
                n *= d
            v = area[:, at:at + n]
            if len(dims) == 2:
                return v.rearrange("p (a b) -> p a b", a=dims[0])
            if len(dims) == 3:
                return v.rearrange("p (a b c) -> p a b c", a=dims[0], b=dims[1])
            return v

        x_tok = view(area_d, 0, NT, D)
        g1 = view(area_e, 0, D)
        hT = view(area_a, 0, KT, T)
        ring = [view(area_a, 8192 + KT * 272 * s, KT, 272) for s in range(2)]
        ycat = view(area_b, 0, 12, T)
        z_s = view(area_b, 4 * T, NT, SW)
        v_tok = view(area_c, 0, NT, 512)
        hconv = view(area_e, 0, 4, CONV_K - 1 + T)
        raw = view(area_d, 0, 6, SCONV_K - 1 + T)
        xtok = view(area_d, 0, NT, SW)
        btok = view(area_d, 4096, NT, P)
        bc0 = 6 * (SCONV_K - 1 + T)
        bc = view(area_d, bc0, 6, T)
        at_ = [view(area_d, bc0 + 512 * s, 4, P) for s in range(2)]
        Lm = [view(area_d, bc0 + 1024 + 512 * s, 4, P) for s in range(2)]
        Wm = [view(area_d, bc0 + 2048 + 512 * s, 4, P) for s in range(2)]
        xD = [view(area_d, bc0 + 3072 + 512 * s, HEADS, HD) for s in range(2)]
        t0 = bc0 + 6 * T
        xdt = [view(area_d, t0 + 512 * s, HEADS, HD) for s in range(2)]
        xdec = [view(area_d, t0 + 1024 + 512 * s, HEADS, HD) for s in range(2)]
        cbm = view(area_d, t0 + 2048, P)
        Hs = view(area_d, t0 + 2048 + 128, 4, HD)
        ty = view(area_d, t0 + 2048 + 384, HEADS, HD)
        qh = view(area_d, 0, 2, 2, T)
        kh = view(area_d, 4096, 2, 2, T)
        Pm = [view(area_d, 8192 + 1024 * s, T) for s in range(2)]
        PT = [view(area_d, 10240 + 1024 * s, T) for s in range(2)]
        otok = view(area_d, 12288, NT, P)
        cumT = view(area_d, 13312, T)
        xn_c = view(area_c, 0, NT, CONV)
        wo_raw = [view(area_a, 2 * WO_RING * D + D * s, D) for s in range(WO_RING)]
        wo_hi = [w_lo[:, D * s:D * s + D] for s in range(WO_RING)]
        wo_lo = [w_lo[:, D * (WO_RING + s):D * (WO_RING + s) + D] for s in range(WO_RING)]
        yo_hi = [y_ring[:, 384 * s:384 * s + 384] for s in range(WO_RING)]
        yo_lo = [y_ring[:, 384 * (WO_RING + s):384 * (WO_RING + s) + 384] for s in range(WO_RING)]
        tiles_of = [range(0, 3), range(3, 6), range(6, NT)]
        k_order = list(range(4, 12)) + list(range(4))
        wo_pieces = [(g, k) for g in range(3) for k in k_order]
        NC = len(wo_pieces)
        x1 = view(area_d, 0, NT, D)
        g2 = view(area_e, 0, D)
        gf = view(area_e, D, D)
        xr = [view(area_e, 2 * D, D), view(area_e, 3 * D, D), view(area_d, 12288, D), view(area_d, 13312, D)]
        hf = [view(area_c, D * s, D) for s in range(2)]
        hfT = [view(area_c, 2 * D + D * s, KT, P) for s in range(2)]
        e0 = 8192
        xg = view(area_d, e0, D)
        ysb = view(area_d, e0 + 2048, D)
        sg = view(area_d, e0 + 3072, FE)
        hh = view(area_d, e0 + 3584, FE)
        raw_gu = [view(area_c, 3 * D, D), view(area_e, 2 * D, D), view(area_e, 3 * D, D), view(area_e, 0, D)]
        raw_dn = [view(area_d, e0 + at, D) for at in (4096, 5120, 6144, 1024)]
        GU, DN = 2 * FE * D // (P * D), FE // P
        ohJ = view(area_d, e0 + 1536, 2 * NT * P // 2).bitcast(BF16).rearrange("p (q j) -> p q j", q=2 * NT)
        yg = view(area_ab, 0, 2 * NT, D)
        outb = view(area_ab, 2 * NT * D, NT, D)

        sm = 0

        def take(*dims):
            nonlocal sm
            v = view(small, sm, *dims)
            n = 1
            for d in dims:
                n *= d
            sm += n
            return v

        fd = take(NT, 16)
        fe = take(NT, 16)
        fu = take(NT, 16)
        fv = take(NT, 16)
        fw = take(NT, 16)
        dt_a = take(NT, HEADS)
        eacum = take(NT, HEADS)
        etot = take(NT, HEADS)
        dtdec = take(NT, HEADS)
        ea = take(HEADS)
        nmax = take(64)
        rsum = take(64)
        rinv = take(64)
        bnst = take(NT, 6)
        bnag = take(NT, 2)
        sm = 0
        lg = take(NT, NG + NE)
        wgt = take(2, NT)
        slot = take(2, NT)
        r4a = take(NT, 4)
        r4b = take(NT, 4)
        selg = take(NT, 4)
        esel = take(NT, 4)
        sel1 = take(NT, 4)
        r1 = take(NT)
        r2 = take(NT)
        r3 = take(NT)
        m1 = take(NT)
        m2 = take(NT)
        gval = take(NT)
        small2 = sb("small2", [P, SW + 64])
        oh = view(area_d, e0 + 0, 2, NT, NE)
        msk = sb("msk", [P, NT, NE], BF16)
        pos = view(area_d, e0 + 384, NT, NE)
        tmp = view(area_d, e0 + 512, NT, NE)
        cmp7 = view(area_d, e0 + 640, NE, NT - 1)
        nb = view(area_d, e0 + 752, NE)
        cb = view(area_d, e0 + 768, NE)
        base = view(area_d, e0 + 784, NE)
        eqB = view(area_d, e0 + 800, 2 * NT, NB + 1)
        ohB = view(area_d, e0 + 2560, NT * 2 * (NB + 1)).bitcast(BF16).rearrange("p (q w b) -> p q w b", q=2 * NT, w=2)
        jf = sb("jf", [P, 2, NT])
        bf = sb("bf", [P, 2, NT])
        slot_i = sb("slot_i", [P, 2, NT], I32)
        jb_i = sb("jb_i", [P, 2, 2, NT], I32)
        cb_i = sb("cb_i", [P, NE + 1], I32)
        idx_i = sb("idx_i", [P, NB + 1], I32)
        idx_now = sb("idx_now", [P, 1], I32)

        ps = ctx.enter_context(nc.psum_tensor("ps", [P, 8, 512], F32))

        def bank(b):
            return ps[:, b, :]

        def two(b):
            return ps[:, b:b + 2, :].rearrange("p b n -> p (b n)")

        hf_d = nc.dram_tensor("hf_scratch", (T, D), F32, kind="Internal").ap()
        y_d = nc.dram_tensor("y_scratch", (SLOTS, D), F32, kind="Internal").ap()

        c_zero = sem("c_zero")
        c_ready = sem("c_ready")
        p_in = sem("p_in")
        pt_in = sem("pt_in")
        g1_in = sem("g1_in")
        x_in = [sem(f"x_in{i}") for i in range(NT)]
        win_in = [sem(f"win_in{s}") for s in range(2)]
        par_ps = sem("par_ps")
        act_step = sem("act_step")
        dve_step = sem("dve_step")
        rms_ok = sem("rms_ok")
        xn_ok = sem("xn_ok")
        hT_ps = sem("hT_ps")
        hT_act = sem("hT_act")
        hT_dve = sem("hT_dve")
        proj_ps = sem("proj_ps")
        proj_act = sem("proj_act")
        proj_dve = sem("proj_dve")
        xbc_ok = sem("xbc_ok")
        xbc_silu = sem("xbc_silu")
        pre_dve = sem("pre_dve")
        pre_act = sem("pre_act")
        pre_ok = sem("pre_ok")
        pre_ps = sem("pre_ps")
        pre_e = sem("pre_e")
        dec_ok = sem("dec_ok")
        cum_ps = sem("cum_ps")
        cum_ok = sem("cum_ok")
        aug_in = [sem(f"aug_in{s}") for s in range(2)]
        aug_one = sem("aug_one")
        xt_ps = sem("xt_ps")
        xt_ok = sem("xt_ok")
        at_ok = sem("at_ok")
        xdt_ok = sem("xdt_ok")
        xdec_ok = sem("xdec_ok")
        xD_ok = sem("xD_ok")
        seg_ps = sem("seg_ps")
        cb_ps = sem("cb_ps")
        st_ps = sem("st_ps")
        yoff_ps = sem("yoff_ps")
        yd_ps = sem("yd_ps")
        L_ok = sem("L_ok")
        cbm_ok = sem("cbm_ok")
        W_ok = sem("W_ok")
        H_ok = sem("H_ok")
        t1_ok = sem("t1_ok")
        t2_ok = sem("t2_ok")
        t3_ok = sem("t3_ok")
        yz_ok = sem("yz_ok")
        sq_ok = sem("sq_ok")
        srms_ok = sem("srms_ok")
        yn_ok = sem("yn_ok")
        yT_ps = sem("yT_ps")
        yT_ok = sem("yT_ok")
        s_ps = sem("s_ps")
        mx_ok = sem("mx_ok")
        p_ok = sem("p_ok")
        pt_ps6 = sem("pt_ps6")
        pt_ps7 = sem("pt_ps7")
        pt_ok6 = sem("pt_ok6")
        pt_ok7 = sem("pt_ok7")
        o_ps = sem("o_ps")
        o_ok = sem("o_ok")
        ot_ps = sem("ot_ps")
        ot_ok = sem("ot_ok")
        dw_ok = sem("dw_ok")
        ln_ps = sem("ln_ps")
        bn_ok = sem("bn_ok")
        lnrms_ok = sem("lnrms_ok")
        lnx_ok = sem("lnx_ok")
        lnT_ps = sem("lnT_ps")
        lnT_ok = sem("lnT_ok")
        wo_in = [sem(f"wo_in{s}") for s in range(WO_RING)]
        wo_split = sem("wo_split")
        wo_ok = sem("wo_ok")
        wo_used = sem("wo_used")
        g2_in = sem("g2_in")
        o2_ps = sem("o2_ps")
        x1_ok = sem("x1_ok")
        rms2_ok = sem("rms2_ok")
        hf_ok = sem("hf_ok")
        hf_out = [sem(f"hf_out{s}") for s in range(2)]
        hfT_ps = sem("hfT_ps")
        hfT_ok = sem("hfT_ok")
        lg_ps = sem("lg_ps")
        rt_dve = sem("rt_dve")
        rt_act = sem("rt_act")
        msk_ok = sem("msk_ok")
        cnt_ps = sem("cnt_ps")
        oh_ok = sem("oh_ok")
        idx_ps = sem("idx_ps")
        route_ok = sem("route_ok")
        gu_in = [sem(f"gu_in{s}") for s in range(len(raw_gu))]
        dn_in = [sem(f"dn_in{s}") for s in range(len(raw_dn))]
        gu_hi = sem("gu_hi")
        gu_lo = sem("gu_lo")
        dn_hi = sem("dn_hi")
        dn_lo = sem("dn_lo")
        ix_ok = sem("ix_ok")
        pool_held = sem("pool_held")
        xg_in = sem("xg_in")
        xg_ps = sem("xg_ps")
        xgT_act = sem("xgT_act")
        xgT_dve = sem("xgT_dve")
        gu_ps = sem("gu_ps")
        sg_ok = sem("sg_ok")
        hh_ok = sem("hh_ok")
        hh_ps = sem("hh_ps")
        hT_act_e = sem("hT_act_e")
        hT_dve_e = sem("hT_dve_e")
        y_ps = sem("y_ps")
        y_act = sem("y_act")
        y_dve = sem("y_dve")
        y_out = sem("y_out")
        yg_in = [sem(f"yg_in{i}") for i in range(NT)]
        x2_ok = sem("x2_ok")
        x2rms_ok = sem("x2rms_ok")
        fin_ok = sem("fin_ok")
        st_out = sem("st_out")

        chunks = [(C_XBC + 256 * m, C_XBC + 256 * m + 128) for m in range(3)]
        chunks += [(C_Z, C_Z + 128)]
        chunks += [(C_GATE + 128 * j, C_A + 128 * j) for j in range(4)]
        chunks += [(C_Z + 256, C_Z + 256 + 128)]
        chunks += [(C_V + 256 * m, C_V + 256 * m + 128) for m in range(2)]
        chunks += [(C_Q + 128 * p, C_K + 128 * p) for p in range(4)]
        M_FD = 3
        jobs = [("xbc", m, s, h) for m in range(3) for s in range(2) for h in range(2)]
        jobs += [("z", M_FD, 0, i) for i in range(NT)]
        jobs += [(("gate", "a")[s], 4 + j, s, h) for j in range(4) for h in range(2) for s in range(2)]
        N_GLU = len(jobs)
        jobs += [("z", 8, 0, i) for i in range(NT)]
        N_PRE = len(jobs)
        jobs += [("v", 9 + m, 0, i) for m in range(2) for i in range(NT)]
        N_SSD = len(jobs)
        jobs += [("qk", 11 + p, s, h) for p in range(4) for s in range(2) for h in range(2)]
        by_dve = [j[0] == "a" for j in jobs]
        n_act = [sum(not d for d in by_dve[:n + 1]) for n in range(len(jobs))]
        n_dve = [sum(by_dve[:n + 1]) for n in range(len(jobs))]
        N_QK = N_SSD
        N_ATT = N_QK + 4

        def job_bank(n):
            return n % 2 if n < N_ATT else 0

        last_job = [max(n for n in range(len(jobs)) if jobs[n][1] == m) for m in range(len(chunks))]

        gate_job = {(jobs[n][1] - 4, jobs[n][3]): n for n in range(len(jobs)) if jobs[n][0] == "gate"}
        fd_job = max(n for n in range(len(jobs)) if jobs[n][1] == M_FD)

        def loads_of(m):
            return 32 * (m // 2 + 1) + (32 if m >= M_FD and m % 2 == M_FD % 2 else 0)

        units = [(p, i, 2 * p + e) for p in range(4) for i in range(NT) for e in range(2)]
        NU = len(units)

        params = [
            (alog[:, :], lambda: A["ssd_A_log"][0].partition_broadcast(P)),
            (dskip[:, :], lambda: A["ssd_D"][0].partition_broadcast(P)),
            (fdb[:, 0:8], lambda: A["fgate_b"][0].partition_broadcast(P)),
            (fdb[:, 8:16], lambda: A["ssd_dt_bias"][0].partition_broadcast(P)),
            (sng[:, :], lambda: A["ssd_norm_g"][0].partition_broadcast(P)),
            (rb[:, 0:NG], lambda: A["router_group_b"][0].partition_broadcast(P)),
            (rb[:, NG:NG + NE], lambda: A["router_expert_b"][0].partition_broadcast(P)),
            (wr[:, :, 0:NG], lambda: A["router_group_w"][0].rearrange("(k p) n -> p k n", p=P)),
            (wr[:, :, NG:NG + NE], lambda: A["router_expert_w"][0].rearrange("(k p) n -> p k n", p=P)),
        ]
        N_PARAMS = len(params)
        crow = view(area_c, 0, CONV)
        srow = view(area_c, CONV, 768)
        sq_junk = view(area_c, 2048, D)

        sgt = view(area_c, 3072, 512)
        sq_junk2 = view(small2, 0, SW)
        sq_junk3 = view(area_d, e0 + 3072, D)
        n_job_end = {}
        piece = {}
        for pair in range(3):
            todo = [(N_ATT + 4 * pair + q, k) for q in range(4) for k in range(KT)]
            for w, take in enumerate(PIECES_OF_UNIT):
                u = 16 * pair + w
                piece[u], todo = todo[:take], todo[take:]
                for n, k in piece[u]:
                    if k == KT - 1:
                        n_job_end[u] = n
        npt7, c7 = [], 0
        for u in range(NU):
            if units[u][1] >= 4:
                c7 += 1
            npt7.append(c7)

        def take_ot(eng, pair):
            eng.wait_ge(ot_ps[1], pair + 1)
            sig(nc.scalar.copy(ycat[:, 4 + pair, :], two(6)), ot_ok)

        eb_f64 = view(small2, 512, NT, HEADS)
        ncumT = view(area_d, 14336, T)

        Y_FILL = 16 * (NB - NE)

        def first_block(eng, e):
            r = eng.alloc_register(f"first{e}")
            eng.reg_alu(r, eng.value_load(cb_i[0:1, e - 1:e], min_val=e, max_val=NB), e, ALU.max)
            return eng.snap(r, min_val=e, max_val=NB)

        def gu_of(w, k):
            v = w[:, 0:8192].rearrange("p (k n) -> p k n", k=KT)
            return v[:, 2 * (k // 2):2 * (k // 2) + 2, FE * (k % 2):FE * (k % 2) + FE]

        def dn_of(w, k):
            return w[:, 8192 + D * k:8192 + D * k + D]

        def gu_raw(c):
            return raw_gu[c % len(raw_gu)].rearrange("p (k n) -> p k n", k=2)

        def one_block(e, first):
            return first[e + 1] < first[e] + 2

        def more_blocks(e, first):
            return first[e + 1] > first[e] + 1

        block = ctx.enter_context(nc.Block())

        @block.sync
        def _(sp):
            def load_chunk(m):
                if m >= 2:
                    sp.wait_ge(proj_ps[1], last_job[m - 2] + 1)
                for half in range(2):
                    c0 = chunks[m][half]
                    sig(sp.dma_start(ring[m % 2][:, :, 128 * half:128 * half + 128],
                                     A["w_in"][0, :, c0:c0 + 128].rearrange("(k p) n -> p k n", p=P)),
                        win_in[m % 2], 16)
                if m == M_FD:
                    for j, c0 in enumerate((C_F, C_DT)):
                        sig(sp.dma_start(ring[m % 2][:, :, 256 + 8 * j:264 + 8 * j],
                                         A["w_in"][0, :, c0:c0 + 8].rearrange("(k p) n -> p k n", p=P)),
                            win_in[m % 2], 16)

            for i in range(NT):
                sig(sp.dma_start(x_tok[:, i, :], A["x"][0, P * i:P * i + P, :]), x_in[i], 16)
            for m in range(len(chunks) - 1):
                load_chunk(m)
            sp.wait_ge(cum_ok[1], 2)
            sp.wait_ge(aug_one[1], 1)
            for p in range(4):
                if p >= 2:
                    if p == 2:
                        load_chunk(len(chunks) - 1)
                    sp.wait_ge(s_ps[1], 16 * (p - 1))
                for e in range(2):
                    sig(sp.dma_start(qh[HD:HD + 1, p % 2, e, :], cumT[2 * p + e:2 * p + e + 1, :]), aug_in[p % 2], 16)
                    sig(sp.dma_start(kh[HD + 1:HD + 2, p % 2, e, :], ncumT[2 * p + e:2 * p + e + 1, :]),
                        aug_in[p % 2], 16)
            sp.wait_ge(proj_ps[1], len(jobs))
            def load_wo(c):
                if c >= WO_RING:
                    sp.wait_ge(wo_ok[1], c - WO_RING + 1)
                k = wo_pieces[c][1]
                sig(sp.dma_start(wo_raw[c % WO_RING], A["w_out"][0, P * k:P * k + P, :]), wo_in[c % WO_RING], 16)

            def load_xr(i):
                if i >= 4:
                    sp.wait_ge(x1_ok[1], i - 3)
                sig(sp.dma_start(xr[i % 4], A["x"][0, P * i:P * i + P, :]), x_in[i], 16)

            for c in range(WO_RING):
                load_wo(c)
            sp.wait_ge(dw_ok[1], 4)
            sig(sp.dma_start(g2, A["norm_ffn"][0].partition_broadcast(P)), g2_in, 16)
            sig(sp.dma_start(gf, A["norm_final"].partition_broadcast(P)), g2_in, 16)
            sp.wait_ge(ot_ps[1], 4)
            for i in range(4):
                load_xr(i)
            for c in range(WO_RING, NC):
                load_wo(c)
                for i in {18: (4, 5, 6), 30: (7,)}.get(c, ()):
                    load_xr(i)

            sp.wait_ge(lg_ps[1], NT)
            def load_gu(e, k0, k1):
                for k in range(k0, k1):
                    c = GU * e + k
                    if c >= len(raw_gu):
                        sp.wait_ge(gu_lo[1], c - len(raw_gu) + 1)
                    w = A[("expert_w_gate", "expert_w_up")[k % 2]][0, e, 256 * (k // 2):256 * (k // 2) + 256, :]
                    sig(sp.dma_start(gu_raw(c), w.rearrange("(k p) n -> p k n", p=P)), gu_in[c % len(raw_gu)], 16)

            def load_dn(e, k0=0, k1=DN):
                for k in range(k0, k1):
                    c = DN * e + k
                    if c >= len(raw_dn):
                        sp.wait_ge(dn_lo[1], c - len(raw_dn) + 1)
                    elif k == DN - 1:
                        sp.wait_ge(route_ok[1], 1)
                    sig(sp.dma_start(raw_dn[c % len(raw_dn)], A["expert_w_down"][0, e, P * k:P * k + P, :]),
                        dn_in[c % len(raw_dn)], 16)

            load_gu(0, 0, GU // 2)
            load_dn(0, 0, DN - 1)
            load_gu(0, GU // 2, GU)
            for e in range(NE):
                if e + 1 < NE:
                    load_gu(e + 1, 0, GU // 2)
                load_dn(e, DN - 1 if e == 0 else 0, DN)
                if e + 1 < NE:
                    load_gu(e + 1, GU // 2, GU)
            for i in range(NT):
                sp.wait_ge(fin_ok[1], i + 1)
                sig(sp.dma_start(out[0, P * i:P * i + P, :], outb[:, i, :]), st_out, 16)
            sp.wait_ge(st_out[1], 16 * NT)

        @block.gpsimd
        def _(pool):
            zeroed = [
                nc.gpsimd.memset(ones[:, :], 1.0),
                nc.gpsimd.memset(ones_b[:, :], 1.0),
                nc.gpsimd.memset(ident[:, :], 0.0),
                nc.gpsimd.memset(identb[:, :], 0.0),
                nc.gpsimd.memset(negmask[:, :], 0.0),
                nc.gpsimd.memset(eps[:, :], EPS),
            ]
            for ins in zeroed:
                n = sig(ins, c_zero)
            pool.wait_ge(c_zero[1], n)

            def select(out_, in_, step, cm, op, fill):
                return nc.gpsimd.affine_select(out=out_, in_=in_, pattern=[[step, P]], compare_op=op, fill=fill,
                                               base=0, channel_multiplier=cm)
            made = [
                select(ident[:, :], ident[:, :], -1, 1, ALU.not_equal, 1.0),
                select(identb[:, :], identb[:, :], -1, 1, ALU.not_equal, 1.0),
                nc.gpsimd.affine_select(out=tri_le[:, :].rearrange("p (a b) -> p a b", a=4),
                                        in_=ones[:, :].unsqueeze(1).broadcast_to([P, 4, P]), pattern=[[P, 4], [1, P]],
                                        compare_op=ALU.is_ge, fill=0.0, base=0, channel_multiplier=-1),
                select(tri_lt[:, :], ones_b[:, :], 1, -1, ALU.is_gt, 0.0),
                select(tri_gt[:, :], ones[:, :], -1, 1, ALU.is_gt, 0.0),
                select(negmask[:, :], negmask[:, :], -1, 1, ALU.is_ge, -BIG),
                nc.gpsimd.iota(iota_j[:, :], pattern=[[1, P]], base=0, channel_multiplier=0,
                               allow_small_or_imprecise_dtypes=True),
                nc.gpsimd.iota(tok_idx[:, :], pattern=[[P, NT]], base=0, channel_multiplier=1,
                               allow_small_or_imprecise_dtypes=True),
                nc.gpsimd.iota(thr[:, :], pattern=[[P, NT - 1]], base=P, channel_multiplier=0,
                               allow_small_or_imprecise_dtypes=True),
                nc.gpsimd.iota(rev4[:, :], pattern=[[-1, 4]], base=4, channel_multiplier=0,
                               allow_small_or_imprecise_dtypes=True),
            ]
            for ins in made:
                sig(ins, c_ready)

            sig(pool.dma_start(crow[0:CONV_K, :], A["conv_dw_w"][0]), pt_in, 16)
            sig(pool.dma_start(crow[CONV_K:CONV_K + 1, :], A["conv_dw_b"]), pt_in, 16)
            sig(pool.dma_start(crow[CONV_K + 1:CONV_K + 2, :], A["conv_ln_g"]), pt_in, 16)
            sig(pool.dma_start(crow[CONV_K + 2:CONV_K + 3, :], A["conv_ln_b"]), pt_in, 16)
            sig(pool.dma_start(srow[0:SCONV_K, :], A["ssd_conv_w"][0]), pt_in, 16)
            sig(pool.dma_start(srow[SCONV_K:SCONV_K + 1, :], A["ssd_conv_b"]), pt_in, 16)
            for dst, src in params:
                sig(pool.dma_start(dst, src()), p_in, 16)

            pool.wait_ge(c_ready[1], len(made))
            pool.wait_ge(p_in[1], 16 * N_PARAMS)
            pool.wait_ge(dec_ok[1], 1)
            pool.wait_ge(xt_ok[1], NT + 2)
            for c in range(NT):
                s = c % 2
                xc = xtok[:, c, :].rearrange("p (h d) -> p h d", h=HEADS)

                def per_head(v):
                    return v.unsqueeze(2).broadcast_to([P, HEADS, HD])
                if c >= 2:
                    pool.wait_ge(yd_ps[1], 2 * (c - 1))
                    pool.wait_ge(st_ps[1], 2 * (c - 1))
                    pool.wait_ge(t3_ok[1], c - 1)
                for g in range(2):
                    if c >= 1:
                        pool.wait_ge(seg_ps[1], 2 * (c - 1) + g + 1)
                    sig(nc.gpsimd.tensor_tensor(
                        at_[g], tri_le[:, 0:P].unsqueeze(1).broadcast_to([P, 4, P]),
                        dt_a[:, c, 4 * g:4 * g + 4].unsqueeze(2).broadcast_to([P, 4, P]), ALU.mult), at_ok)
                sig(nc.gpsimd.tensor_tensor(xdec[s], xc, per_head(dtdec[:, c, :]), ALU.mult), xdec_ok)
                sig(nc.gpsimd.tensor_tensor(xdt[s], xc, per_head(fv[:, c, 8:16]), ALU.mult), xdt_ok)
                sig(nc.gpsimd.tensor_tensor(xD[s], xc, per_head(dskip[:, :]), ALU.mult), xD_ok)

            pool.wait_ge(route_ok[1], 1)
            for s in range(2):
                pool.wait_ge(hf_out[s][1], 16 * (NT // 2))
            last = pool.value_load(cb_i[0:1, NE:NE + 1], min_val=NE - 1, max_val=NB - 1)

            def gather(g):
                nc.gpsimd.tensor_copy(idx_now[:, :], idx_i[:, bass.ds(g, 1)]).then_inc(ix_ok[1], 1)
                pool.wait_ge(ix_ok[1], g + 1)
                pool.sem_inc(pool_held[1], 1)
                nc.gpsimd.indirect_dma_start(
                    out=xg, out_offset=None, in_=hf_d, in_offset=bass.IndirectOffsetOnAxis(ap=idx_now[:, 0:1], axis=0)
                ).then_inc(xg_in[1], 16)

            gather(0)
            with pool.Fori(1, last + 2) as g:
                pool.wait_ge(xg_ps[1], g)
                pool.wait_ge(xg_in[1], 16 * g)
                pool.sem_inc(pool_held[1], 1)
                gather(g)
            pool.wait_ge(xg_in[1], 16 * last + 32)
            pool.wait_ge(y_out[1], 16 * last + 16 + Y_FILL)
            pool.sem_inc(pool_held[1], 1)
            for i in range(NT):
                for k in range(2):
                    sig(nc.gpsimd.indirect_dma_start(
                        out=yg[:, 2 * i + k, :], out_offset=None, in_=y_d,
                        in_offset=bass.IndirectOffsetOnAxis(ap=slot_i[:, k, i:i + 1], axis=0)), yg_in[i], 16)

        @block.scalar
        def _(act):
            A_ = nc.scalar.activation
            sig(act.dma_start(g1, A["norm_mix"][0].partition_broadcast(P)), g1_in, 16)

            act.wait_ge(c_zero[1], 6)
            A_(warm[:, :], eps[:, :], ACT.Sqrt)
            for i in range(NT + 1):
                if i < NT:
                    act.wait_ge(x_in[i][1], 16)
                    n = sig(A_(sq_junk, x_tok[:, i, :], ACT.Square, accum_out=ssq[:, i:i + 1]), act_step)
                    act.wait_ge(act_step[1], n)
                    sig(A_(rms[:, i:i + 1], ssq[:, i:i + 1], ACT.Sqrt, bias=eps[:, :], scale=1.0 / D), rms_ok)
                if i >= 1:
                    j = i - 1
                    act.wait_ge(hT_ps[1], 2 * j + 1)
                    sig(nc.scalar.copy(hT[:, 0:4, P * j:P * j + P],
                                       bank(2 * (j % 3)).rearrange("p (k t) -> p k t", k=4)), hT_act)

            def take_job(n):
                kind, m, s, h = jobs[n]
                b = bank(job_bank(n))
                act.wait_ge(proj_ps[1], n + 1)
                if kind == "xbc":
                    ct = 2 * m + s
                    sig(nc.scalar.copy(raw[:, ct, SCONV_K - 1 + 512 * h:SCONV_K - 1 + 512 * h + 512], b), proj_act)
                elif kind == "gate":
                    q = 2 * (m - 4) + h
                    if q >= 1:
                        act.wait_ge(proj_dve[1], q)
                    sig(A_(sgt, b, ACT.Sigmoid), proj_act)
                elif kind == "z":
                    c0 = 256 * (m != M_FD)
                    ins = A_(z_s[:, h, c0:c0 + 256], b[:, 0:256], ACT.Silu)
                    if m == M_FD:
                        ins = nc.scalar.copy(fd[:, h, :], b[:, 256:272])
                    sig(ins, proj_act)
                elif kind == "v":
                    sig(nc.scalar.copy(v_tok[:, h, 256 * (m - 9):256 * (m - 9) + 256], b[:, 0:256]), proj_act)
                elif kind == "qk":
                    pair = m - 11
                    if pair >= 2 and s == 0 and h == 0:
                        act.wait_ge(s_ps[1], 16 * (pair - 1))
                    dst = (qh, kh)[s]
                    for e in range(2):
                        o = dst[0:HD, pair % 2, e, 512 * h:512 * h + 512]
                        i_ = b[HD * e:HD * e + HD, :]
                        ins = A_(o, i_, ACT.Copy, scale=HD ** -0.5) if s == 0 else nc.scalar.copy(o, i_)
                    sig(ins, proj_act)

            for n in range(N_GLU):
                if not by_dve[n]:
                    take_job(n)
                if n == gate_job[(1, 1)]:
                    act.wait_ge(p_in[1], 16 * N_PARAMS)
                    sig(A_(ea, alog[:, :], ACT.Exp), pre_act)
                    act.wait_ge(pre_dve[1], 1)
                    sig(A_(fe, fe, ACT.Exp), pre_act)
                    act.wait_ge(pre_dve[1], 2)
                    sig(A_(fw, fu, ACT.Ln), pre_act)
            for ct in range(6):
                act.wait_ge(xbc_ok[1], ct + 1)
                sig(A_(bc[:, ct, :], bc[:, ct, :], ACT.Silu), xbc_silu)
            for n in range(N_GLU, N_PRE):
                take_job(n)
            for c in range(NT):
                act.wait_ge(xt_ps[1], c + 1)
                sig(nc.scalar.copy(xtok[:, c, :], bank(2 + c % 2)), xt_ok)
            for q in range(2):
                act.wait_ge(xt_ps[1], NT + q + 1)
                sig(nc.scalar.copy(btok[:, 4 * q:4 * q + 4, :], bank(4 + q).rearrange("p (c n) -> p c n", c=4)), xt_ok)
            act.wait_ge(pre_ps[1], 1)
            ac = bank(6)[:, 0:64].rearrange("p (c h) -> p c h", c=NT)
            tt = bank(6)[:, 64:128].rearrange("p (c h) -> p c h", c=NT)
            sig(A_(eacum, ac, ACT.Exp), pre_e)
            sig(A_(etot, tt, ACT.Exp), pre_e)
            act.wait_ge(pre_dve[1], 3)
            sig(A_(dtdec, dtdec, ACT.Exp), pre_e)

            for u in range(2 * NT):
                act.wait_ge(seg_ps[1], u + 1)
                if u >= 2:
                    act.wait_ge(W_ok[1], u - 1)
                sig(A_(Lm[u % 2], bank(2 + u % 2).rearrange("p (h t) -> p h t", h=4), ACT.Exp), L_ok)
                take_job(N_PRE + u)
                if u >= 3 and u % 2 == 1:
                    c = (u - 3) // 2
                    act.wait_ge(yz_ok[1], c + 1)
                    if c >= 1:
                        act.wait_ge(sq_ok[1], c)
                    sig(A_(sq_junk2, z_s[:, c, :], ACT.Square, accum_out=ssq[:, c:c + 1]), sq_ok)
            act.wait_ge(yz_ok[1], NT)
            act.wait_ge(sq_ok[1], NT - 1)
            n = sig(A_(sq_junk2, z_s[:, NT - 1, :], ACT.Square, accum_out=ssq[:, NT - 1:NT]), sq_ok)
            act.wait_ge(sq_ok[1], n)
            sig(A_(rms[:, :], ssq[:, :], ACT.Sqrt, bias=eps[:, :], scale=1.0 / SW), srms_ok)
            for n in range(N_QK, N_ATT):
                if n == N_QK:
                    act.wait_ge(yz_ok[1], NT)
                    act.wait_ge(yd_ps[1], 2 * NT)
                take_job(n)
            for c in range(NT):
                act.wait_ge(yT_ps[1], c + 1)
                sig(nc.scalar.copy(ycat[:, 8:12, P * c:P * c + P], bank(2 + c % 2).rearrange("p (k t) -> p k t", k=4)),
                    yT_ok)

            def exp_(u):
                p, i, h = units[u]
                L = P * (i + 1)
                act.wait_ge(mx_ok[1], u + 1)
                if u >= 2:
                    act.wait_ge(pt_ps6[1], u - 1)
                    if npt7[u - 2]:
                        act.wait_ge(pt_ps7[1], npt7[u - 2])
                sig(A_(Pm[u % 2][:, 0:L], two(2 + 2 * (u % 2))[:, 0:L], ACT.Exp, bias=nmax[:, u:u + 1],
                       accum_out=rsum[:, u:u + 1]), p_ok)

            for b in range(NE, NB):
                sig(act.dma_start(y_d[P * b:P * b + P, :].rearrange("p (r c) -> p r c", c=P),
                                  ones[:, :].unsqueeze(1).broadcast_to([P, D // P, P])), y_out, 16)
            for u in range(NU + 1):
                if u < NU:
                    exp_(u)
                    if n_job_end.get(u) is not None:
                        take_job(n_job_end[u])
                if u >= 17 and u % 16 == 1:
                    take_ot(act, u // 16 - 1)
                if u >= 1:
                    i = units[u - 1][1]
                    L = min(512, P * (i + 1))
                    act.wait_ge(pt_ps6[1], u)
                    if u >= 3:
                        act.wait_ge(o_ps[1], u - 2)
                    sig(nc.scalar.copy(PT[(u - 1) % 2][:, 0:L], bank(6)[:, 0:L]), pt_ok6)
            take_ot(act, 3)

            def split_wo(c):
                g, k = wo_pieces[c]
                t0, n = P * tiles_of[g][0], P * len(tiles_of[g])
                act.wait_ge(wo_in[c % WO_RING][1], 16 * (c // WO_RING + 1))
                q = c - WO_RING
                if q >= 0:
                    if wo_pieces[q][1] == k_order[-1]:
                        act.wait_ge(o2_ps[1], tiles_of[wo_pieces[q][0]][-1] + 1)
                    else:
                        act.wait_ge(wo_used[1], q + 1 - q // 12)
                nc.scalar.copy(wo_hi[c % WO_RING], wo_raw[c % WO_RING])
                sig(nc.scalar.copy(yo_hi[c % WO_RING][:, 0:n], ycat[:, k, t0:t0 + n]), wo_split)

            act.wait_ge(o_ps[1], NU)
            act.wait_ge(pt_ps7[1], npt7[-1])
            act.wait_ge(ot_ok[1], 4)
            for c in range(WO_RING):
                split_wo(c)
            act.wait_ge(bn_ok[1], NT)
            sig(A_(rms[:, :], bnag[:, :, 1], ACT.Sqrt, bias=eps[:, :]), lnrms_ok)
            for q in range(8):
                h, j = q // 4, q % 4
                act.wait_ge(lnT_ps[1], q + 1)
                sig(A_(ycat[:, j, 512 * h:512 * h + 512], bank(4 * h + j), ACT.Silu,
                       bias=convp[:, j, CONV_K + 2:CONV_K + 3], scale=convp[:, j, CONV_K + 1:CONV_K + 2]), lnT_ok)

            def squares(i):
                act.wait_ge(x1_ok[1], i + 1)
                n = sig(A_(sq_junk3, x1[:, i, :], ACT.Square, accum_out=ssq[:, i:i + 1]), act_step)
                act.wait_ge(act_step[1], n)
                sig(A_(rms[:, i:i + 1], ssq[:, i:i + 1], ACT.Sqrt, bias=eps[:, :], scale=1.0 / D), rms2_ok)

            def store_hf(i):
                act.wait_ge(hf_ok[1], i + 1)
                sig(act.dma_start(hf_d[P * i:P * i + P, :], hf[i % 2]), hf_out[i % 2], 16)

            def take_hfT(j):
                act.wait_ge(hfT_ps[1], j + 1)
                if j >= 2:
                    act.wait_ge(lg_ps[1], j - 1)
                sig(nc.scalar.copy(hfT[j % 2].rearrange("p k t -> p (k t)"), two(4)), hfT_ok)

            for c in range(WO_RING, NC):
                if c == len(k_order) - 4:
                    act.wait_ge(lnT_ok[1], 8)
                for g in range(2):
                    if c == 12 * (g + 1) + WO_RING - 1:
                        for i in tiles_of[g]:
                            squares(i)
                if c > 24 and (c - 25) % 2 == 0:
                    store_hf((c - 25) // 2)
                if c >= 28 and c % 2 == 0:
                    take_hfT((c - 28) // 2)
                split_wo(c)
            take_hfT(4)
            squares(6)
            take_hfT(5)
            squares(7)
            store_hf(6)
            take_hfT(6)
            store_hf(7)
            take_hfT(7)
            def split_gu(e, k0, k1):
                for k in range(k0, k1):
                    c = GU * e + k
                    act.wait_ge(gu_in[c % len(raw_gu)][1], 16 * (c // len(raw_gu) + 1))
                    nc.scalar.copy(gu_of(w_hi, k), gu_raw(c)).then_inc(gu_hi[1], 1)

            def split_dn(e, g):
                if e > 0:
                    act.wait_ge(y_ps[1], g + 2)
                for k in range(DN):
                    c = DN * e + k
                    act.wait_ge(dn_in[c % len(raw_dn)][1], 16 * (c // len(raw_dn) + 1))
                    nc.scalar.copy(dn_of(w_hi, k), raw_dn[c % len(raw_dn)]).then_inc(dn_hi[1], 1)

            act.wait_ge(o2_ps[1], NT)
            split_gu(0, 0, GU)
            act.wait_ge(rt_dve[1], 1)
            sig(A_(r4a, r4a, ACT.Exp), rt_act)
            act.wait_ge(rt_dve[1], 2)
            sig(A_(r3, r3, ACT.Exp), rt_act)

            act.wait_ge(route_ok[1], 1)

            def silu_gate(g):
                act.wait_ge(gu_ps[1], g + 1)
                act.wait_ge(hh_ok[1], g)
                A_(sg, bank(0), ACT.Silu).then_inc(sg_ok[1], 1)

            def take_xT(g):
                act.wait_ge(xg_ps[1], g + 1)
                act.wait_ge(gu_ps[1], g)
                nc.scalar.copy(xT_hi[:, :], two(2)).then_inc(xgT_act[1], 1)

            def take_hT(g):
                act.wait_ge(hh_ps[1], g + 1)
                act.wait_ge(y_ps[1], g + 1)
                nc.scalar.copy(hT_hi[:, :], bank(4)).then_inc(hT_act_e[1], 1)

            def take_y(g):
                act.wait_ge(y_ps[1], g + 2)
                act.wait_ge(y_out[1], 16 * g + Y_FILL)
                nc.scalar.copy(ysb[:, 0:512], bank(5)).then_inc(y_act[1], 1)
                act.wait_ge(y_act[1], g + 2)
                act.wait_ge(y_dve[1], g + 2)
                act.dma_start(y_d[bass.ds(P * g, P), :], ysb).then_inc(y_out[1], 16)

            act.sem_inc(y_act[1], 1)
            act.wait_ge(y_out[1], Y_FILL)
            first = [0]
            take_xT(0)
            for e in range(NE):
                def block(g, head):
                    if head and e > 0:
                        act.wait_ge(gu_ps[1], g)
                        split_gu(e, 0, GU // 2)
                    if not (head and e == 0):
                        take_hT(g - 1)
                    if e > 2 or (e == 2 and not head):
                        take_y(g - 2)
                    if head and e > 0:
                        split_gu(e, GU // 2, GU)
                        with act.If(one_block(e - 1, first)):
                            split_dn(e - 1, g - 2)
                    silu_gate(g)
                    take_xT(g + 1)
                    if e < 2 and not (head and e == 0):
                        take_y(g - 1)

                first.append(first_block(act, e + 1))
                block(first[e], True)
                with act.If(more_blocks(e, first)):
                    split_dn(e, first[e] - 1)
                    with act.Fori(first[e] + 1, first[e + 1]) as g:
                        block(g, False)
            last = act.value_load(cb_i[0:1, NE:NE + 1], min_val=NE - 1, max_val=NB - 1)
            with act.If(one_block(NE - 1, first)):
                split_dn(NE - 1, last - 1)
            take_hT(last)
            take_y(last - 1)
            take_y(last)
            for i in range(NT):
                act.wait_ge(x2_ok[1], i + 1)
                n = sig(A_(sq_junk3, x1[:, i, :], ACT.Square, accum_out=ssq[:, i:i + 1]), act_step)
                act.wait_ge(act_step[1], n)
                sig(A_(rms[:, i:i + 1], ssq[:, i:i + 1], ACT.Sqrt, bias=eps[:, :], scale=1.0 / D), x2rms_ok)

        @block.vector
        def _(dve):
            V = nc.vector

            def link(ins):
                dve.wait_ge(dve_step[1], sig(ins, dve_step))

            dve.wait_ge(g1_in[1], 16)
            for i in range(NT + 1):
                if i < NT:
                    dve.wait_ge(rms_ok[1], i + 1)
                    link(V.reciprocal(rstd[:, i:i + 1], rms[:, i:i + 1]))
                    sig(V.scalar_tensor_tensor(out=x_tok[:, i, :], in0=x_tok[:, i, :], scalar=rstd[:, i:i + 1],
                                               in1=g1, op0=ALU.mult, op1=ALU.mult), xn_ok)
                if i >= 1:
                    j = i - 1
                    dve.wait_ge(hT_ps[1], 2 * j + 2)
                    sig(V.tensor_copy(hT[:, 4:8, P * j:P * j + P],
                                      bank(2 * (j % 3) + 1).rearrange("p (k t) -> p k t", k=4)), hT_dve)
            dve.wait_ge(par_ps[1], 1)
            V.tensor_copy(convp[:, :, :], bank(6)[:, 0:4 * (CONV_K + 3)].rearrange("p (j c) -> p j c", j=4))
            link(V.tensor_copy(sconvp[:, :, :], bank(7)[:, 0:6 * (SCONV_K + 1)].rearrange("p (j c) -> p j c", j=6)))
            dve.wait_ge(xn_ok[1], NT)
            V.memset(raw[:, :, 0:SCONV_K - 1], 0.0)
            link(V.memset(hconv[:, :, 0:CONV_K - 1], 0.0))

            def xs_conv(ct):
                dve.wait_ge(proj_act[1], n_act[2 * ct + 1])
                link(V.tensor_scalar(bc[:, ct, :], raw[:, ct, 0:T], sconvp[:, ct, 0:1],
                                     sconvp[:, ct, SCONV_K:SCONV_K + 1], ALU.mult, ALU.add))
                for k in range(1, SCONV_K):
                    ins = V.scalar_tensor_tensor(out=bc[:, ct, :], in0=raw[:, ct, k:k + T],
                                                 scalar=sconvp[:, ct, k:k + 1], in1=bc[:, ct, :],
                                                 op0=ALU.mult, op1=ALU.add)
                    if k < SCONV_K - 1:
                        link(ins)
                    else:
                        sig(ins, xbc_ok)

            def glu(j, h):
                n = gate_job[(j, h)]
                dve.wait_ge(proj_act[1], n_act[n])
                dve.wait_ge(proj_ps[1], n + 2)
                sig(V.tensor_tensor(hconv[:, j, CONV_K - 1 + 512 * h:CONV_K - 1 + 512 * h + 512],
                                    bank(job_bank(n + 1)), sgt, ALU.mult), proj_dve)

            def dw(j, k0, k1):
                if k0 == 0:
                    dve.wait_ge(proj_dve[1], 2 * j + 2)
                for k in range(k0, k1):
                    o = ycat[:, j, :]
                    if k == 0:
                        ins = V.tensor_scalar(o, hconv[:, j, 0:T], convp[:, j, 0:1], convp[:, j, CONV_K:CONV_K + 1],
                                              ALU.mult, ALU.add)
                    else:
                        ins = V.scalar_tensor_tensor(out=o, in0=hconv[:, j, k:k + T], scalar=convp[:, j, k:k + 1],
                                                     in1=o, op0=ALU.mult, op1=ALU.add)
                    if k < CONV_K - 1:
                        link(ins)
                    else:
                        sig(ins, dw_ok)

            for ct in range(6):
                xs_conv(ct)
            glu(0, 0)
            glu(0, 1)
            glu(1, 0)
            glu(1, 1)

            dve.wait_ge(proj_act[1], n_act[fd_job])
            dve.wait_ge(p_in[1], 16 * N_PARAMS)
            link(V.tensor_tensor(fd, fd, fdb[:, :].unsqueeze(1).broadcast_to([P, NT, 16]), ALU.add))
            link(V.tensor_scalar(fd[:, :, 0:8], fd[:, :, 0:8], -1.0, None, ALU.mult))
            link(V.tensor_scalar(fu, fd, -1.0, None, ALU.mult))
            sig(V.tensor_tensor(fe, fd, fu, ALU.min), pre_dve)
            dve.wait_ge(pre_act[1], 2)
            sig(V.tensor_scalar(fu, fe, 1.0, None, ALU.add), pre_dve)
            dve.wait_ge(pre_dve[1], 2)
            link(V.tensor_scalar(fv, fu, -1.0, None, ALU.add))
            dve.wait_ge(pre_act[1], 3)
            link(V.tensor_scalar(fu, fv, 1e-30, None, ALU.max))
            link(V.reciprocal(fu, fu))
            link(V.tensor_tensor(fu, fu, fe, ALU.mult))
            link(V.tensor_tensor(fw, fw, fu, ALU.mult))
            link(V.scalar_tensor_tensor(out=fv, in0=fv, scalar=0.0, in1=fe, op0=ALU.is_equal, op1=ALU.mult))
            link(V.tensor_tensor(fw, fw, fv, ALU.add))
            link(V.scalar_tensor_tensor(out=fv, in0=fd, scalar=0.0, in1=fw, op0=ALU.max, op1=ALU.add))
            link(V.tensor_scalar(fv[:, :, 0:8], fv[:, :, 0:8], -1.0, None, ALU.mult))
            dve.wait_ge(pre_act[1], 3)
            link(V.tensor_scalar(ea, ea, -1.0, None, ALU.mult))
            sig(V.tensor_tensor(dt_a, fv[:, :, 8:16], ea.unsqueeze(1).broadcast_to([P, NT, HEADS]), ALU.mult), pre_ok)

            dw(0, 0, 10)
            glu(2, 0)
            dw(0, 10, 20)
            glu(2, 1)
            dw(0, 20, 31)
            glu(3, 0)
            dw(1, 0, 10)
            glu(3, 1)
            dw(1, 10, 18)

            dw(1, 18, 31)
            dw(2, 0, 4)

            dve.wait_ge(pre_e[1], 2)
            link(V.tensor_copy(eb_f64, bank(6)[:, 0:64].rearrange("p (c h) -> p c h", c=NT)))
            sig(V.tensor_tensor(dtdec, bank(6)[:, 64:128].rearrange("p (c h) -> p c h", c=NT), eb_f64,
                                ALU.subtract), pre_dve)
            dve.wait_ge(pre_e[1], 3)
            sig(V.tensor_tensor(dtdec, dtdec, fv[:, :, 8:16], ALU.mult), dec_ok)
            sig(V.memset(Hs, 0.0), H_ok)
            dve.wait_ge(H_ok[1], 1)

            for u in range(2 * NT):
                c, g = u // 2, u % 2
                lo = HD * g
                dve.wait_ge(cb_ps[1], u + 1)
                if u == 0:
                    dve.wait_ge(c_ready[1], 10)
                n = sig(V.tensor_tensor(cbm, bank(4)[:, 0:P], tri_le[:, 0:P], ALU.mult), cbm_ok)
                dve.wait_ge(cbm_ok[1], n)
                dve.wait_ge(L_ok[1], u + 1)
                if u >= 2:
                    dve.wait_ge(yd_ps[1], u - 1)
                sig(V.tensor_tensor(Wm[u % 2], Lm[u % 2], cbm.unsqueeze(1).broadcast_to([P, 4, P]), ALU.mult), W_ok)
                dve.wait_ge(yoff_ps[1], u + 1)
                dve.wait_ge(st_ps[1], u + 1)
                link(V.tensor_tensor(Hs[lo:lo + HD], Hs[lo:lo + HD],
                                     etot[lo:lo + HD, c, 4 * g:4 * g + 4].unsqueeze(2).broadcast_to([HD, 4, HD]),
                                     ALU.mult))
                nH = sig(V.tensor_tensor(Hs[lo:lo + HD], bank(7)[lo:lo + HD, 0:256].rearrange("p (h d) -> p h d", h=4),
                                    Hs[lo:lo + HD], ALU.add), H_ok)
                if g == 1:
                    n = sig(V.tensor_tensor(ty, bank(6).rearrange("p (h d) -> p h d", h=HEADS),
                                            eacum[:, c, :].unsqueeze(2).broadcast_to([P, HEADS, HD]), ALU.mult), t1_ok)
                    dve.wait_ge(t1_ok[1], n)
                    dve.wait_ge(yd_ps[1], u + 1)
                    n = sig(V.tensor_tensor(ty, bank(5).rearrange("p (h d) -> p h d", h=HEADS), ty, ALU.add), t2_ok)
                    dve.wait_ge(t2_ok[1], n)
                    dve.wait_ge(xD_ok[1], c + 1)
                    n = sig(V.tensor_tensor(ty, ty, xD[c % 2], ALU.add), t3_ok)
                    dve.wait_ge(t3_ok[1], n)
                    sig(V.tensor_tensor(z_s[:, c, :], ty.rearrange("p h d -> p (h d)"), z_s[:, c, :], ALU.mult), yz_ok)
            dve.wait_ge(srms_ok[1], 1)
            link(V.reciprocal(rstd[:, :], rms[:, :]))
            for c in range(NT):
                sig(V.scalar_tensor_tensor(out=z_s[:, c, :], in0=z_s[:, c, :], scalar=rstd[:, c:c + 1], in1=sng[:, :],
                                           op0=ALU.mult, op1=ALU.mult), yn_ok)
            dve.wait_ge(cum_ps[1], 1)
            dve.wait_ge(yz_ok[1], NT)
            dve.wait_ge(yd_ps[1], 2 * NT)
            V.memset(qh[HD:HD + 2].rearrange("p a b t -> p (a b t)"), 1.0)
            sig(V.memset(kh[HD:HD + 2].rearrange("p a b t -> p (a b t)"), 1.0), aug_one)
            sig(V.tensor_copy(cumT[0:HEADS, :], two(6)[0:HEADS, :]), cum_ok)
            sig(V.tensor_scalar(ncumT[0:HEADS, :], two(6)[0:HEADS, :], -1.0, None, ALU.mult), cum_ok)

            late_taps = [(2, k, k + 1) for k in range(4, CONV_K)] + [(3, k, k + 1) for k in range(CONV_K)]
            for u in range(NU + 2):
                if u < NU:
                    L = P * (units[u][1] + 1)
                    dve.wait_ge(s_ps[1], u + 1)
                    sig(V.tensor_reduce(nmax[:, u:u + 1], two(2 + 2 * (u % 2))[:, 0:L], AX_X, ALU.max, negate=True),
                        mx_ok)
                    if u < len(late_taps):
                        dw(*late_taps[u])
                if u >= 2:
                    w = u - 2
                    p, i, h = units[w]
                    dve.wait_ge(p_ok[1], w + 1)
                    link(V.reciprocal(rinv[:, w:w + 1], rsum[:, w:w + 1]))
                    dve.wait_ge(o_ps[1], w + 1)
                    if w >= 16 and w % 16 == 0:
                        dve.wait_ge(ot_ps[1], p)
                    e = HD * (h % 2)
                    sig(V.tensor_scalar(otok[:, i, e:e + HD], bank(1)[:, 0:HD], rinv[:, w:w + 1], None, ALU.mult),
                        o_ok)
                if 1 <= u <= NU and units[u - 1][1] >= 4:
                    i = units[u - 1][1]
                    dve.wait_ge(pt_ps7[1], npt7[u - 1])
                    if u >= 3:
                        dve.wait_ge(o_ps[1], u - 2)
                    sig(V.tensor_copy(PT[(u - 1) % 2][:, 512:P * (i + 1)], bank(7)[:, 0:P * (i + 1) - 512]), pt_ok7)

            for i in range(NT):
                dve.wait_ge(ln_ps[1], i + 1)
                link(V.bn_stats(bnst[:, i, :], bank(i)))
                sig(V.bn_aggr(bnag[:, i, :], bnst[:, i, :]), bn_ok)
            dve.wait_ge(lnrms_ok[1], 1)
            link(V.reciprocal(rstd[:, :], rms[:, :]))
            for i in range(NT):
                sig(V.tensor_scalar(xn_c[:, i, :], bank(i), bnag[:, i, 0:1], rstd[:, i:i + 1], ALU.subtract,
                                    ALU.mult), lnx_ok)

            def split_wo(c):
                g, k = wo_pieces[c]
                r = c % WO_RING
                t0, n = P * tiles_of[g][0], P * len(tiles_of[g])
                dve.wait_ge(wo_split[1], c + 1)
                V.tensor_tensor(wo_lo[r], wo_raw[r], wo_hi[r].bitcast(F32), ALU.subtract)
                sig(V.tensor_tensor(yo_lo[r][:, 0:n], ycat[:, k, t0:t0 + n], yo_hi[r][:, 0:n].bitcast(F32),
                                    ALU.subtract), wo_ok)

            def add_x(i, j):
                dve.wait_ge(o2_ps[1], i + 1)
                dve.wait_ge(x_in[i][1], 32)
                sig(V.tensor_tensor(x1[:, i, :], two(2 * j), xr[i % 4], ALU.add), x1_ok)

            def norm(i):
                dve.wait_ge(rms2_ok[1], i + 1)
                link(V.reciprocal(rstd[:, i:i + 1], rms[:, i:i + 1]))
                if i >= 2:
                    dve.wait_ge(hf_out[i % 2][1], 16 * (i // 2))
                    dve.wait_ge(hfT_ps[1], i - 1)
                sig(V.scalar_tensor_tensor(out=hf[i % 2], in0=x1[:, i, :], scalar=rstd[:, i:i + 1], in1=g2,
                                           op0=ALU.mult, op1=ALU.mult), hf_ok)

            for c in range(NC):
                if c == WO_RING:
                    dve.wait_ge(g2_in[1], 32)
                for g in range(2):
                    if c == 12 * (g + 1) + WO_RING - 1:
                        for j, i in enumerate(tiles_of[g]):
                            add_x(i, j)
                if c >= 24 and c % 2 == 0:
                    norm((c - 24) // 2)
                split_wo(c)
            add_x(6, 0)
            add_x(7, 1)
            norm(6)
            norm(7)

            def split_gu(e, k0, k1):
                for k in range(k0, k1):
                    c = GU * e + k
                    dve.wait_ge(gu_hi[1], c + 1)
                    V.tensor_tensor(gu_of(w_lo, k), gu_raw(c), gu_of(w_hi, k).bitcast(F32),
                                    ALU.subtract).then_inc(gu_lo[1], 1)

            def split_dn(e, g):
                for k in range(DN):
                    c = DN * e + k
                    dve.wait_ge(dn_hi[1], c + 1)
                    V.tensor_tensor(dn_of(w_lo, k), raw_dn[c % len(raw_dn)], dn_of(w_hi, k).bitcast(F32),
                                    ALU.subtract).then_inc(dn_lo[1], 1)

            def b4(v):
                return v.unsqueeze(2).broadcast_to([P, NT, 4])

            dve.wait_ge(lg_ps[1], NT)
            link(V.tensor_tensor(lg, bank(6)[:, 0:NT * 20].rearrange("p (i c) -> p i c", i=NT),
                                 rb[:, :].unsqueeze(1).broadcast_to([P, NT, NG + NE]), ALU.add))
            gl = lg[:, :, 0:NG]

            def first_max(vals, best, sel):
                link(V.tensor_reduce(best, vals, AX_X, ALU.max))
                link(V.tensor_tensor(sel, vals, b4(best), ALU.is_equal))
                link(V.tensor_tensor(sel, sel, rev4[:, :].unsqueeze(1).broadcast_to([P, NT, 4]), ALU.mult))
                link(V.tensor_reduce(r2, sel, AX_X, ALU.max))
                link(V.tensor_tensor(sel, sel, b4(r2), ALU.is_equal))

            first_max(gl, r1, selg)
            sig(V.tensor_tensor(r4a, gl, b4(r1), ALU.subtract), rt_dve)
            t4 = tmp.rearrange("p i (g e) -> p i g e", g=NG)
            for g in range(NG):
                link(V.tensor_tensor(t4[:, :, g, :], lg[:, :, NG + EPG * g:NG + EPG * g + EPG],
                                     b4(selg[:, :, g]), ALU.mult))
            link(V.tensor_tensor(r4b, t4[:, :, 0, :], t4[:, :, 1, :], ALU.add))
            link(V.tensor_tensor(esel, t4[:, :, 2, :], t4[:, :, 3, :], ALU.add))
            link(V.tensor_tensor(esel, esel, r4b, ALU.add))
            first_max(esel, m1, sel1)
            link(V.scalar_tensor_tensor(out=esel, in0=sel1, scalar=-3.0e38, in1=esel, op0=ALU.mult, op1=ALU.add))
            first_max(esel, m2, r4b)
            sig(V.tensor_tensor(r3, m2, m1, ALU.subtract), rt_dve)
            for k, sel in enumerate((sel1, r4b)):
                o4 = oh[:, k].rearrange("p i (g e) -> p i g e", g=NG)
                for g in range(NG):
                    link(V.tensor_tensor(o4[:, :, g, :], sel, b4(selg[:, :, g]), ALU.mult))
            sig(V.tensor_tensor(msk[:, :, :], oh[:, 0], oh[:, 1], ALU.add), msk_ok)
            split_gu(0, 0, 1)
            dve.wait_ge(cnt_ps[1], 1)
            V.tensor_copy(pos, bank(0)[:, 0:P].rearrange("p (i e) -> p i e", i=NT))
            link(V.tensor_copy(nb, bank(0)[:, P:P + NE]))
            link(V.tensor_tensor(cmp7, nb.unsqueeze(2).broadcast_to([P, NE, NT - 1]),
                                 thr[:, :].unsqueeze(1).broadcast_to([P, NE, NT - 1]), ALU.is_gt))
            link(V.tensor_reduce(nb, cmp7, AX_X, ALU.add))
            link(V.tensor_scalar(nb, nb, 1.0, None, ALU.add))
            link(V.tensor_tensor_scan(cb, ones[:, 0:NE], nb, 0.0, ALU.mult, ALU.add))
            V.tensor_copy(cb_i[:, 0:NE], cb)
            V.tensor_scalar(cb_i[:, NE:NE + 1], cb[:, NE - 1:NE], -1.0, None, ALU.add)
            link(V.tensor_tensor(base, cb, nb, ALU.subtract))
            link(V.tensor_scalar(base, base, float(P), None, ALU.mult))
            link(V.tensor_tensor(pos, pos, base.unsqueeze(1).broadcast_to([P, NT, NE]), ALU.add))
            for k in range(2):
                link(V.tensor_tensor(tmp, pos, oh[:, k], ALU.mult))
                link(V.tensor_reduce(slot[:, k], tmp, AX_X, ALU.add))
            link(V.tensor_copy(slot_i[:, :, :], slot))
            V.tensor_scalar(jb_i[:, 0], slot_i[:, :, :], P - 1, None, ALU.bitwise_and)
            link(V.tensor_scalar(jb_i[:, 1], slot_i[:, :, :], 7, None, ALU.arith_shift_right))
            V.tensor_copy(jf[:, :, :], jb_i[:, 0])
            link(V.tensor_copy(bf[:, :, :], jb_i[:, 1]))
            link(V.tensor_tensor(eqB, iota_j[:, 0:NB + 1].unsqueeze(1).broadcast_to([P, 2 * NT, NB + 1]),
                                 bf[:, :, :].rearrange("p k i -> p (k i)").unsqueeze(2)
                                 .broadcast_to([P, 2 * NT, NB + 1]), ALU.is_equal))
            for k in range(2):
                V.tensor_tensor(ohB[:, NT * k:NT * k + NT, 0], eqB[:, NT * k:NT * k + NT],
                                iota_j[:, 0:NT].unsqueeze(2).broadcast_to([P, NT, NB + 1]), ALU.mult)
            V.tensor_scalar(ohB[:, :, 1], eqB, tok_idx[:, 0:1], None, ALU.mult)
            sig(V.tensor_tensor(ohJ, iota_j[:, :].unsqueeze(1).broadcast_to([P, 2 * NT, P]),
                                jf[:, :, :].rearrange("p k i -> p (k i)").unsqueeze(2).broadcast_to([P, 2 * NT, P]),
                                ALU.is_equal), oh_ok)
            split_gu(0, 1, 3)
            dve.wait_ge(idx_ps[1], 1)
            link(V.tensor_copy(eqB[:, 0, :], bank(1)[:, NB + 1:2 * (NB + 1)]))
            sig(V.scalar_tensor_tensor(out=idx_i[:, :], in0=bank(1)[:, 0:NB + 1], scalar=float(P), in1=eqB[:, 0, :],
                                       op0=ALU.mult, op1=ALU.add), route_ok)

            split_gu(0, 3, GU)
            dve.wait_ge(rt_act[1], 1)
            link(V.tensor_reduce(r1, r4a, AX_X, ALU.add))
            link(V.reciprocal(gval, r1))
            dve.wait_ge(rt_act[1], 2)
            link(V.tensor_scalar(r2, r3, 1.0, None, ALU.add))
            link(V.reciprocal(r2, r2))
            link(V.tensor_tensor(wgt[:, 0], r2, gval, ALU.mult))
            link(V.tensor_tensor(wgt[:, 1], wgt[:, 0], r3, ALU.mult))

            dve.wait_ge(route_ok[1], 1)

            def take_xT(g):
                dve.wait_ge(xgT_act[1], g + 1)
                V.tensor_tensor(xT_lo[:, :], two(2), xT_hi[:, :].bitcast(F32), ALU.subtract).then_inc(xgT_dve[1], 1)

            def mul_up(g):
                dve.wait_ge(sg_ok[1], g + 1)
                dve.wait_ge(hh_ps[1], g)
                V.tensor_tensor(hh, bank(1), sg, ALU.mult).then_inc(hh_ok[1], 1)

            def take_hT(g):
                dve.wait_ge(hT_act_e[1], g + 1)
                V.tensor_tensor(hT_lo[:, :], bank(4), hT_hi[:, :].bitcast(F32), ALU.subtract).then_inc(hT_dve_e[1], 1)

            def take_y(g):
                dve.wait_ge(y_ps[1], g + 2)
                dve.wait_ge(y_out[1], 16 * g + Y_FILL)
                V.tensor_copy(ysb[:, 512:1024], bank(6)).then_inc(y_dve[1], 1)

            dve.sem_inc(y_dve[1], 1)
            first = [0]
            take_xT(0)
            for e in range(NE):
                def block(g, head):
                    if head and e > 0:
                        split_gu(e, 0, GU // 2)
                    if not (head and e == 0):
                        take_hT(g - 1)
                    if e > 2 or (e == 2 and not head):
                        take_y(g - 2)
                    if head and e > 0:
                        split_gu(e, GU // 2, GU)
                        with dve.If(one_block(e - 1, first)):
                            split_dn(e - 1, g - 2)
                    mul_up(g)
                    take_xT(g + 1)
                    if e < 2 and not (head and e == 0):
                        take_y(g - 1)

                first.append(first_block(dve, e + 1))
                block(first[e], True)
                with dve.If(more_blocks(e, first)):
                    split_dn(e, first[e] - 1)
                    with dve.Fori(first[e] + 1, first[e + 1]) as g:
                        block(g, False)
            last = dve.value_load(cb_i[0:1, NE:NE + 1], min_val=NE - 1, max_val=NB - 1)
            with dve.If(one_block(NE - 1, first)):
                split_dn(NE - 1, last - 1)
            take_hT(last)
            take_y(last - 1)
            take_y(last)

            for i in range(NT + 1):
                if i < NT:
                    dve.wait_ge(yg_in[i][1], 32)
                    if i == 0:
                        dve.wait_ge(route_ok[1], 1)
                    link(V.scalar_tensor_tensor(out=x1[:, i, :], in0=yg[:, 2 * i, :], scalar=wgt[:, 0, i:i + 1],
                                                in1=x1[:, i, :], op0=ALU.mult, op1=ALU.add))
                    sig(V.scalar_tensor_tensor(out=x1[:, i, :], in0=yg[:, 2 * i + 1, :], scalar=wgt[:, 1, i:i + 1],
                                               in1=x1[:, i, :], op0=ALU.mult, op1=ALU.add), x2_ok)
                if i >= 1:
                    j = i - 1
                    dve.wait_ge(x2rms_ok[1], j + 1)
                    link(V.reciprocal(rstd[:, j:j + 1], rms[:, j:j + 1]))
                    sig(V.scalar_tensor_tensor(out=outb[:, j, :], in0=x1[:, j, :], scalar=rstd[:, j:j + 1], in1=gf,
                                               op0=ALU.mult, op1=ALU.mult), fin_ok)

        @block.tensor
        def _(pe):
            M = nc.tensor.matmul
            TR = nc.tensor.transpose
            pe.wait_ge(c_ready[1], 10)
            for i in range(NT):
                pe.wait_ge(xn_ok[1], i + 1)
                if i >= 3:
                    pe.wait_ge(hT_act[1], i - 2)
                    pe.wait_ge(hT_dve[1], i - 2)
                for k in range(KT):
                    b = 2 * (i % 3) + k // 4
                    ins = TR(bank(b)[:, P * (k % 4):P * (k % 4) + P], x_tok[:, i, P * k:P * k + P], ident[:, :])
                    if k % 4 == 3:
                        sig(ins, hT_ps)

            def proj(n, k0=0, k1=KT):
                kind, m, s, h = jobs[n]
                b = bank(job_bank(n))
                if k0 == 0:
                    before = [q for q in range(n) if job_bank(q) == job_bank(n)]
                    if before:
                        q = before[-1]
                        if by_dve[q]:
                            pe.wait_ge(proj_dve[1], n_dve[q])
                        else:
                            pe.wait_ge(proj_act[1], n_act[q])
                    pe.wait_ge(win_in[m % 2][1], loads_of(m))
                for k in range(k0, k1):
                    if kind in ("z", "v"):
                        w = 272 if m == M_FD else 256
                        ins = M(b[:, 0:w], hT[:, k, P * h:P * h + P], ring[m % 2][:, k, 0:w],
                                start=(k == 0), stop=(k == KT - 1))
                    else:
                        ins = M(b, ring[m % 2][:, k, P * s:P * s + P], hT[:, k, 512 * h:512 * h + 512],
                                start=(k == 0), stop=(k == KT - 1))
                if k1 == KT:
                    sig(ins, proj_ps)

            pe.wait_ge(pt_in[1], 96)
            for j in range(4):
                TR(bank(6)[:, 34 * j:34 * j + 34], crow[0:34, P * j:P * j + P], ident[0:34, 0:34])
            for j in range(6):
                ins = TR(bank(7)[:, 5 * j:5 * j + 5], srow[0:5, P * j:P * j + P], ident[0:5, 0:5])
            sig(ins, par_ps)
            pe.wait_ge(hT_act[1], NT)
            pe.wait_ge(hT_dve[1], NT)
            pe.wait_ge(p_in[1], 16 * N_PARAMS)
            for n in range(N_PRE):
                proj(n)

            pe.wait_ge(xbc_silu[1], 6)
            for c in range(NT):
                if c >= 2:
                    pe.wait_ge(xt_ok[1], c - 1)
                for j in range(4):
                    ins = TR(bank(2 + c % 2)[:, P * j:P * j + P], bc[:, j, P * c:P * c + P], ident[:, :])
                sig(ins, xt_ps)
            for q in range(2):
                for j in range(4):
                    c = 4 * q + j
                    ins = TR(bank(4 + q)[:, P * j:P * j + P], bc[:, 4, P * c:P * c + P], ident[:, :])
                sig(ins, xt_ps)
            pe.wait_ge(pre_ok[1], 1)
            af = dt_a.rearrange("p c h -> p (c h)")
            M(bank(6)[:, 0:64], tri_le[:, 0:P], af, start=True, stop=True)
            sig(M(bank(6)[:, 64:128], ones[:, :], af, start=True, stop=True), pre_ps)

            pe.wait_ge(xt_ok[1], NT + 2)
            pe.wait_ge(dec_ok[1], 1)
            for u in range(2 * NT):
                c, g = u // 2, u % 2
                lo = HD * g
                pe.wait_ge(at_ok[1], u + 1)
                if u >= 2:
                    pe.wait_ge(L_ok[1], u - 1)
                sig(M(bank(2 + g), tri_gt[:, :], at_[g].rearrange("p h t -> p (h t)"), start=True, stop=True), seg_ps)
                if u >= 1:
                    pe.wait_ge(cbm_ok[1], u)
                sig(M(bank(4)[:, 0:P], bc[lo:lo + HD, 4, P * c:P * c + P], bc[lo:lo + HD, 5, P * c:P * c + P],
                      start=True, stop=True), cb_ps)
                pe.wait_ge(xdec_ok[1], c + 1)
                pe.wait_ge(H_ok[1], u + 1)
                sig(M(ps[lo:lo + HD, 7, 0:256], btok[:, c, lo:lo + HD],
                      xdec[c % 2][:, 4 * g:4 * g + 4, :].rearrange("p h d -> p (h d)"), start=True, stop=True), st_ps)
                if g == 0 and c >= 1:
                    pe.wait_ge(t1_ok[1], c)
                sig(M(bank(6)[:, 256 * g:256 * g + 256], bc[lo:lo + HD, 5, P * c:P * c + P],
                      Hs[lo:lo + HD].rearrange("p h d -> p (h d)"), start=True, stop=True), yoff_ps)
                n = N_PRE + u
                proj(n)
                pe.wait_ge(W_ok[1], u + 1)
                pe.wait_ge(xdt_ok[1], c + 1)
                if g == 0 and c >= 1:
                    pe.wait_ge(t2_ok[1], c)
                for q in range(4):
                    h = 4 * g + q
                    ins = M(bank(5)[:, HD * h:HD * h + HD], Wm[u % 2][:, q, :], xdt[c % 2][:, h, :],
                            start=True, stop=True)
                sig(ins, yd_ps)
            pe.wait_ge(t1_ok[1], NT)
            pe.wait_ge(H_ok[1], 2 * NT + 1)
            lf = fv[:, :, 0:8]
            for half in range(2):
                o = ps[0:HEADS, 6 + half, :]
                order = list(range(4 * half + 3, -1, -1))
                for j in order:
                    q = j - 4 * half
                    if q >= 0:
                        last = M(o[:, P * q:512], lf[:, j, :], tri_le[:, 0:512 - P * q], start=(j == order[0]),
                                 stop=(j == 0), skip_group_check=True)
                    else:
                        last = M(o, lf[:, j, :], ones[:, :].unsqueeze(1).broadcast_to([P, 4, P]), start=False,
                                 stop=(j == 0), skip_group_check=True)
            sig(last, cum_ps)
            for n in range(N_QK, N_ATT):
                proj(n)
            for c in range(NT):
                pe.wait_ge(yn_ok[1], c + 1)
                if c >= 2:
                    pe.wait_ge(yT_ok[1], c - 1)
                for j in range(4):
                    ins = TR(bank(2 + c % 2)[:, P * j:P * j + P], z_s[:, c, P * j:P * j + P], ident[:, :])
                sig(ins, yT_ps)
            pe.wait_ge(yT_ok[1], NT)
            pe.wait_ge(cum_ok[1], 2)

            def scores(u):
                p, i, h = units[u]
                e, s = h % 2, p % 2
                L = P * (i + 1)
                if u % 16 == 0:
                    pe.wait_ge(proj_act[1], n_act[N_QK + 4 * p + 3])
                    pe.wait_ge(aug_in[s][1], 64 * (p // 2 + 1))
                if u >= 2:
                    pe.wait_ge(p_ok[1], u - 1)
                b = 2 + 2 * (u % 2)
                for c0 in range(0, L, 512):
                    n = min(512, L - c0)
                    diag = c0 + n == L
                    o = bank(b + c0 // 512)
                    if diag:
                        M(o[:, n - P:n], identb[:, :], negmask[:, :], start=True, stop=False, skip_group_check=True)
                    last = M(o[:, 0:n], qh[0:HD + 2, s, e, P * i:P * i + P], kh[0:HD + 2, s, e, c0:c0 + n],
                             start=not diag, stop=True, skip_group_check=True)
                sig(last, s_ps)

            def turn(u):
                i = units[u][1]
                pe.wait_ge(p_ok[1], u + 1)
                if u >= 1:
                    pe.wait_ge(pt_ok6[1], u)
                if u >= 1 and u % 16 == 0:
                    pe.wait_ge(ot_ok[1], u // 16)
                for j in range(i + 1):
                    if j == 4 and npt7[u] >= 2:
                        pe.wait_ge(pt_ok7[1], npt7[u] - 1)
                    ins = TR(bank(6 + j // 4)[:, P * (j % 4):P * (j % 4) + P], Pm[u % 2][:, P * j:P * j + P], ident[:, :])
                    if j == min(i, 3):
                        sig(ins, pt_ps6)
                if i >= 4:
                    sig(ins, pt_ps7)

            def values(u):
                p, i, h = units[u]
                pe.wait_ge(pt_ok6[1], u + 1)
                if i >= 4:
                    pe.wait_ge(pt_ok7[1], npt7[u])
                if u >= 1:
                    pe.wait_ge(o_ok[1], u)
                for j in range(i + 1):
                    ins = M(bank(1)[:, 0:HD], PT[u % 2][:, P * j:P * j + P], v_tok[:, j, HD * h:HD * h + HD],
                            start=(j == 0), stop=(j == i))
                    if j == i:
                        sig(ins, o_ps)
                    yield

            def turn_out(pair, turned):
                pe.wait_ge(o_ok[1], 16 * pair + 16)
                pe.wait_ge(pt_ok6[1], turned + 1)
                pe.wait_ge(pt_ok7[1], npt7[turned])
                for i in range(NT):
                    ins = TR(bank(6 + i // 4)[:, P * (i % 4):P * (i % 4) + P], otok[:, i, :], ident[:, :])
                sig(ins, ot_ps)

            def weave(long_, short):
                for n, step in enumerate(long_):
                    step()
                    if n > 0:
                        next(short, None)
                        next(short, None)
                for _ in short:
                    pass

            def long_steps(u):
                for n, k in piece.get(u, []):
                    yield lambda n=n, k=k: proj(n, k, k + 1)

            for u in range(NU + 2):
                if u < NU:
                    scores(u)
                weave(long_steps(u), values(u - 2) if u >= 2 else iter(()))
                if u >= 2 and (u - 2) % 16 == 15:
                    turn_out((u - 2) // 16, u - 2)
                if 1 <= u <= NU:
                    turn(u - 1)

            pe.wait_ge(o_ok[1], NU)
            pe.wait_ge(ot_ok[1], 4)
            pe.wait_ge(dw_ok[1], 4)
            for i in range(NT):
                for j in range(4):
                    ins = TR(bank(i)[:, P * j:P * j + P], ycat[:, j, P * i:P * i + P], ident[:, :])
                sig(ins, ln_ps)
            for q in range(8):
                h, j = q // 4, q % 4
                pe.wait_ge(lnx_ok[1], 4 * h + 4)
                for t in range(4):
                    ins = TR(bank(q)[:, P * t:P * t + P], xn_c[:, 4 * h + t, P * j:P * j + P], ident[:, :])
                sig(ins, lnT_ps)

            def turn_hf(j):
                pe.wait_ge(hf_ok[1], j + 1)
                pe.wait_ge(x1_ok[1], 6)
                if j >= 1:
                    pe.wait_ge(hfT_ok[1], j)
                for k in range(KT):
                    ins = TR(bank(4 + k // 4)[:, P * (k % 4):P * (k % 4) + P], hf[j % 2][:, P * k:P * k + P],
                             ident[:, :])
                sig(ins, hfT_ps)

            def logits(j):
                pe.wait_ge(hfT_ok[1], j + 1)
                for k in range(KT):
                    ins = M(bank(6)[:, 20 * j:20 * j + 20], hfT[j % 2][:, k, :], wr[:, k, :],
                            start=(k == 0), stop=(k == KT - 1))
                sig(ins, lg_ps)

            pe.wait_ge(lnT_ok[1], 8)
            for c in range(NC):
                g, k = wo_pieces[c]
                r = c % WO_RING
                pe.wait_ge(wo_ok[1], c + 1)
                for j, i in enumerate(tiles_of[g]):
                    if g > 0 and k == k_order[0]:
                        pe.wait_ge(x1_ok[1], tiles_of[g - 1][j] + 1)
                    xh, xl = yo_hi[r][:, P * j:P * j + P], yo_lo[r][:, P * j:P * j + P]
                    for n in range(2):
                        wh, wl = wo_hi[r][:, 512 * n:512 * n + 512], wo_lo[r][:, 512 * n:512 * n + 512]
                        M(bank(2 * j + n), xh, wh, start=(k == k_order[0]), stop=False)
                        M(bank(2 * j + n), xh, wl, start=False, stop=False)
                        ins = M(bank(2 * j + n), xl, wh, start=False, stop=(k == k_order[-1]))
                    if k == k_order[-1] and j < len(tiles_of[g]) - 1:
                        sig(ins, o2_ps)
                sig(ins, o2_ps if k == k_order[-1] else wo_used)
                if c >= 24 and c % 2 == 0:
                    j = (c - 24) // 2
                    if j >= 1:
                        logits(j - 1)
                    turn_hf(j)
            logits(5)
            turn_hf(6)
            logits(6)
            turn_hf(7)
            logits(7)

            pe.wait_ge(msk_ok[1], 1)
            for i in range(NT - 1):
                M(bank(0)[:, NE * (i + 1):P], ones_b[:, :], msk[:, i, :].unsqueeze(1).broadcast_to([P, NT - 1 - i, NE]),
                  start=(i == 0), stop=False, skip_group_check=True)
            M(bank(0)[:, 0:P], tri_lt[:, :], msk[:, :, :].rearrange("p i e -> p (i e)"), start=False, stop=True,
              skip_group_check=True)
            for i in range(NT):
                ins = M(bank(0)[:, P:P + NE], ones_b[:, :], msk[:, i, :], start=(i == 0), stop=(i == NT - 1))
            sig(ins, cnt_ps)
            pe.wait_ge(oh_ok[1], 1)
            for q in range(2 * NT):
                ins = M(bank(1)[:, 0:2 * (NB + 1)], ohJ[:, q, :], ohB[:, q].rearrange("p w b -> p (w b)"), start=(q == 0), stop=(q == 2 * NT - 1))
            sig(ins, idx_ps)

            pe.wait_ge(route_ok[1], 1)

            def turn_x(g):
                pe.wait_ge(xg_in[1], 16 * g + 16)
                pe.wait_ge(xgT_act[1], g)
                pe.wait_ge(xgT_dve[1], g)
                for k in range(KT):
                    ins = TR(bank(2 + k // 4)[:, P * (k % 4):P * (k % 4) + P], xg[:, P * k:P * k + P], ident[:, :])
                ins.then_inc(xg_ps[1], 1)

            def products(b, x_hi, x_lo, at, k, K):
                for n in range(2):
                    wh, wl = w_hi[:, at + 512 * n:at + 512 * n + 512], w_lo[:, at + 512 * n:at + 512 * n + 512]
                    M(bank(b + n), x_hi, wh, start=(k == 0), stop=False)
                    M(bank(b + n), x_hi, wl, start=False, stop=False)
                    ins = M(bank(b + n), x_lo, wh, start=False, stop=(k == K - 1))
                return ins

            def gate_up(g, e):
                pe.wait_ge(xgT_act[1], g + 1)
                pe.wait_ge(xgT_dve[1], g + 1)
                pe.wait_ge(sg_ok[1], g)
                pe.wait_ge(hh_ok[1], g)
                for k in range(KT):
                    if e is not None and k % 2 == 0:
                        pe.wait_ge(gu_lo[1], GU * e + k + 2)
                    ins = products(0, xT_hi[:, P * k:P * k + P], xT_lo[:, P * k:P * k + P], 2 * FE * k, k, KT)
                ins.then_inc(gu_ps[1], 1)

            def turn_h(g):
                pe.wait_ge(hh_ok[1], g + 1)
                pe.wait_ge(hT_act_e[1], g)
                pe.wait_ge(hT_dve_e[1], g)
                for k in range(FE // P):
                    ins = TR(bank(4)[:, P * k:P * k + P], hh[:, P * k:P * k + P], ident[:, :])
                ins.then_inc(hh_ps[1], 1)

            def down(g, e):
                pe.wait_ge(hT_act_e[1], g + 1)
                pe.wait_ge(hT_dve_e[1], g + 1)
                pe.wait_ge(dn_lo[1], DN * e + DN)
                pe.wait_ge(y_act[1], g + 1)
                pe.wait_ge(y_dve[1], g + 1)
                for k in range(FE // P):
                    ins = products(5, hT_hi[:, P * k:P * k + P], hT_lo[:, P * k:P * k + P], 8192 + D * k, k, FE // P)
                ins.then_inc(y_ps[1], 1)

            pe.sem_inc(y_ps[1], 1)
            first = [0]
            turn_x(0)
            for e in range(NE):
                first.append(first_block(pe, e + 1))
                gate_up(first[e], e)
                turn_x(first[e] + 1)
                if e > 0:
                    down(first[e] - 1, e - 1)
                turn_h(first[e])
                with pe.If(first[e + 1] > first[e] + 1):
                    with pe.Fori(first[e] + 1, first[e + 1]) as g:
                        gate_up(g, None)
                        turn_x(g + 1)
                        down(g - 1, e)
                        turn_h(g)
            last = pe.value_load(cb_i[0:1, NE:NE + 1], min_val=NE - 1, max_val=NB - 1)
            down(last, NE - 1)


_INS = ["x", "norm_mix", "w_in", "conv_dw_w", "conv_dw_b", "conv_ln_g", "conv_ln_b", "fgate_b", "ssd_conv_w",
        "ssd_conv_b", "ssd_dt_bias", "ssd_A_log", "ssd_D", "ssd_norm_g", "w_out", "norm_ffn", "router_group_w",
        "router_group_b", "router_expert_w", "router_expert_b", "expert_w_gate", "expert_w_up", "expert_w_down",
        "norm_final"]
_OUTS = [((1, T, D), "float32")]


def kernel(**inputs):
    import numpy as _np
    import concourse.bacc as _bacc
    from concourse.bass_utils import run_bass_kernel_spmd as _run

    nc = _bacc.Bacc("TRN2", target_bir_lowering=False, num_devices=1)
    arrays, args = {}, {}
    for name in _INS:
        a = _np.ascontiguousarray(inputs[name])
        arrays[f"in_{name}_dram"] = a
        args[name] = nc.dram_tensor(f"in_{name}_dram", a.shape, mybir.dt.from_np(a.dtype), kind="ExternalInput").ap()
    outs = []
    for i, (shape, dtype) in enumerate(_OUTS):
        dt = mybir.dt.from_np(_np.dtype(dtype))
        outs.append(nc.dram_tensor(f"out_{i}_dram", shape, dt, kind="ExternalOutput").ap())
    trunk(nc, args, outs[0])
    r = _run(nc, [arrays], core_ids=[0])
    got = tuple(r.results[0][f"out_{i}_dram"] for i in range(len(_OUTS)))
    return got[0]
```
